# Optimizing a Trainium2 kernel written in Bass

```python
import math
import jax, jax.numpy as jnp
from jax import lax
import numpy as np

'''Hybrid autoregressive decoder trunk of DEPTH post-norm (DeepNorm) layers.
Layer i uses token mixer (i mod 2): even layers = sliding-window grouped-query
attention (window 128) with learned per-head sinks, odd layers = differential
attention. In every layer the token mixer heads run side by side with a 4-head
cross-attention into memory tokens: one combined input projection whose columns
are split among the mixer heads and the memory-query heads, head outputs are
concatenated and mapped by one output projection. Then x <- LN(alpha*x + mix),
followed by a DeepSeek-V3 style MoE (sigmoid routing, group-limited top-k, one
shared expert) and x <- LN(alpha*x + moe). Positions enter only through ALiBi.
Inputs: x (BATCH, SEQ, D_MODEL), mem (BATCH, MEM_LEN, D_MODEL), weights.
Output: (BATCH, SEQ, D_MODEL).
'''

D_MODEL = 1024
BATCH = 1
SEQ = 256
DEPTH = 2

N_MIXERS = 2
HEAD_DIM = 64
MEM_LEN = 256
MEM_HEADS = 4
MIX_HEADS = D_MODEL // HEAD_DIM - MEM_HEADS
SWA_Q_HEADS = MIX_HEADS
SWA_KV_HEADS = MIX_HEADS // 4
WINDOW = 128
BLOCK = 128
DIFF_HEADS = MIX_HEADS // 2
DIFF_V_DIM = 2 * HEAD_DIM
N_EXPERTS = 64
TOP_K = 8
N_GROUPS = 8
TOPK_GROUPS = 4
EXPERT_HIDDEN = D_MODEL // 4
SHARED_HIDDEN = D_MODEL // 4
ROUTED_SCALE = 2.5
MOE_BLOCK = 256
DN_ALPHA = (2.0 * DEPTH) ** 0.25
DN_BETA = (8.0 * DEPTH) ** -0.25
LN_EPS = 1e-5
NEG = -1e30

kernel_name = 'hybrid_swa_sink_diffattn_memxattn_moe_deepnorm'

def alibi_slopes(n):
    def pow2_slopes(m):
        start = 2.0 ** (-8.0 / m)
        return [start ** (i + 1) for i in range(m)]
    if (n & (n - 1)) == 0:
        s = pow2_slopes(n)
    else:
        c = 2 ** int(math.floor(math.log2(n)))
        s = pow2_slopes(c) + pow2_slopes(2 * c)[0::2][: n - c]
    return jnp.asarray(np.array(s, dtype=np.float32))

def layer_norm(x, g, b):
    xf = x.astype(jnp.float32)
    mu = jnp.mean(xf, axis=-1, keepdims=True)
    var = jnp.mean(jnp.square(xf - mu), axis=-1, keepdims=True)
    y = (xf - mu) * lax.rsqrt(var + LN_EPS) * g.astype(jnp.float32) + b.astype(jnp.float32)
    return y.astype(x.dtype)

def rms_norm(x, g):
    xf = x.astype(jnp.float32)
    y = xf * lax.rsqrt(jnp.mean(jnp.square(xf), axis=-1, keepdims=True) + LN_EPS)
    return (y * g.astype(jnp.float32)).astype(x.dtype)

def swa_sink_attention(q, k, v, sinks, slopes):
    B, S = q.shape[:2]
    nb = S // BLOCK
    g = SWA_Q_HEADS // SWA_KV_HEADS
    qb = q.reshape(B, nb, BLOCK, SWA_KV_HEADS, g, HEAD_DIM)
    kb = k.reshape(B, nb, BLOCK, SWA_KV_HEADS, HEAD_DIM)
    vb = v.reshape(B, nb, BLOCK, SWA_KV_HEADS, HEAD_DIM)
    shift = lambda t: jnp.concatenate([jnp.zeros_like(t[:, :1]), t[:, :-1]], axis=1)
    kk = jnp.concatenate([shift(kb), kb], axis=2)
    vv = jnp.concatenate([shift(vb), vb], axis=2)
    qi = jnp.arange(BLOCK)[:, None]
    kj = jnp.arange(2 * BLOCK)[None, :]
    dist = qi - kj + BLOCK
    kpos = (jnp.arange(nb)[:, None] - 1) * BLOCK + jnp.arange(2 * BLOCK)[None, :]
    valid = ((dist >= 0) & (dist < WINDOW))[None] & (kpos >= 0)[:, None, :]
    s = jnp.einsum('bnqhgd,bnkhd->bnhgqk', qb, kk).astype(jnp.float32) * (HEAD_DIM ** -0.5)
    s = s - slopes.reshape(SWA_KV_HEADS, g)[:, :, None, None] * dist.astype(jnp.float32)
    s = jnp.where(valid[None, :, None, None], s, NEG)
    sink = sinks.astype(jnp.float32).reshape(SWA_KV_HEADS, g)[None, None, :, :, None, None]
    m = jnp.maximum(jnp.max(s, axis=-1, keepdims=True), sink)
    p = jnp.exp(s - m)
    p = p / (jnp.sum(p, axis=-1, keepdims=True) + jnp.exp(sink - m))
    out = jnp.einsum('bnhgqk,bnkhd->bnqhgd', p.astype(v.dtype), vv)
    return out.reshape(B, S, SWA_Q_HEADS * HEAD_DIM)

def diff_attention(q, k, v, lam, slopes):
    B, S = q.shape[:2]
    nb = S // BLOCK
    qblocks = jnp.swapaxes(q.reshape(B, nb, BLOCK, DIFF_HEADS, 2, HEAD_DIM), 0, 1)
    kpos = jnp.arange(S)

    def one_block(args):
        qblk, n = args
        qpos = n * BLOCK + jnp.arange(BLOCK)
        dist = qpos[:, None] - kpos[None, :]
        s = jnp.einsum('bqhcd,bkhcd->bhcqk', qblk, k).astype(jnp.float32) * (HEAD_DIM ** -0.5)
        s = s - slopes[None, :, None, None, None] * dist.astype(jnp.float32)
        s = jnp.where(dist >= 0, s, NEG)
        p = jax.nn.softmax(s, axis=-1)
        a = p[:, :, 0] - lam * p[:, :, 1]
        return jnp.einsum('bhqk,bkhe->bqhe', a.astype(v.dtype), v)

    out = lax.map(one_block, (qblocks, jnp.arange(nb)))
    return jnp.swapaxes(out, 0, 1).reshape(B, S, DIFF_HEADS, DIFF_V_DIM)

def memory_attention(q, mem, w_kv):
    B, S = q.shape[:2]
    kv = mem @ w_kv
    km, vm = jnp.split(kv, 2, axis=-1)
    km = km.reshape(B, MEM_LEN, MEM_HEADS, HEAD_DIM)
    vm = vm.reshape(B, MEM_LEN, MEM_HEADS, HEAD_DIM)
    s = jnp.einsum('bshd,bmhd->bhsm', q, km).astype(jnp.float32) * (HEAD_DIM ** -0.5)
    p = jax.nn.softmax(s, axis=-1)
    out = jnp.einsum('bhsm,bmhd->bshd', p.astype(vm.dtype), vm)
    return out.reshape(B, S, MEM_HEADS * HEAD_DIM)

def moe_ffn(x, w_router, router_bias, w_gate, w_up, w_down, ws_gate, ws_up, ws_down):
    B, S, D = x.shape
    n = B * S
    xt = x.reshape(n, D)
    aff = jax.nn.sigmoid((xt @ w_router).astype(jnp.float32))
    sel = aff + router_bias.astype(jnp.float32)
    per_group = N_EXPERTS // N_GROUPS
    gscore = jnp.sum(lax.top_k(sel.reshape(n, N_GROUPS, per_group), 2)[0], axis=-1)
    gidx = lax.top_k(gscore, TOPK_GROUPS)[1]
    gmask = jnp.sum(jax.nn.one_hot(gidx, N_GROUPS, dtype=jnp.float32), axis=1) > 0
    emask = jnp.repeat(gmask, per_group, axis=1)
    eidx = lax.top_k(jnp.where(emask, sel, -jnp.inf), TOP_K)[1]
    gates = jnp.take_along_axis(aff, eidx, axis=-1)
    gates = gates / jnp.sum(gates, axis=-1, keepdims=True) * ROUTED_SCALE

    nk = n * TOP_K
    flat_e = eidx.reshape(-1)
    flat_t = jnp.repeat(jnp.arange(n, dtype=jnp.int32), TOP_K)
    flat_g = gates.reshape(-1)
    order = jnp.argsort(flat_e)
    se, st, sg = flat_e[order], flat_t[order], flat_g[order]
    counts = jnp.bincount(flat_e, length=N_EXPERTS)
    padded = (counts + MOE_BLOCK - 1) // MOE_BLOCK * MOE_BLOCK
    starts = jnp.cumsum(counts) - counts
    pends = jnp.cumsum(padded)
    pstarts = pends - padded
    dest = pstarts[se] + (jnp.arange(nk) - starts[se])
    n_rows = (nk + N_EXPERTS * (MOE_BLOCK - 1) + MOE_BLOCK - 1) // MOE_BLOCK * MOE_BLOCK
    n_blocks = n_rows // MOE_BLOCK
    row_t = jnp.full((n_rows,), n, jnp.int32).at[dest].set(st)
    row_g = jnp.zeros((n_rows,), jnp.float32).at[dest].set(sg)
    block_e = jnp.clip(jnp.searchsorted(pends, jnp.arange(n_blocks) * MOE_BLOCK, side='right'), 0, N_EXPERTS - 1)
    x_pad = jnp.concatenate([xt, jnp.zeros((1, D), xt.dtype)], axis=0)

    def expert_block(args):
        rows, e = args
        xb = x_pad[rows]
        h = jax.nn.silu(xb @ w_gate[e]) * (xb @ w_up[e])
        return h @ w_down[e]

    yb = lax.map(expert_block, (row_t.reshape(n_blocks, MOE_BLOCK), block_e)).reshape(n_rows, D)
    routed = jax.ops.segment_sum(yb * row_g[:, None].astype(yb.dtype), row_t, num_segments=n + 1)[:n]
    shared = (jax.nn.silu(xt @ ws_gate) * (xt @ ws_up)) @ ws_down
    return (routed + shared).reshape(B, S, D)

def setup_inputs(seed: int = 0) -> dict:
    key = jax.random.key(seed)
    ks = jax.random.split(key, 24)
    D = D_MODEL
    n_a = (DEPTH + 1) // 2
    n_b = DEPTH // 2
    sd = D ** -0.5
    nrm = lambda k, shape, scale: jax.random.normal(k, shape, jnp.float32) * scale
    qa, kva = SWA_Q_HEADS * HEAD_DIM, SWA_KV_HEADS * HEAD_DIM
    qb, vb = DIFF_HEADS * 2 * HEAD_DIM, DIFF_HEADS * DIFF_V_DIM
    mq = MEM_HEADS * HEAD_DIM
    w_in_a = jnp.concatenate([nrm(ks[0], (n_a, D, qa + kva), sd),
                              nrm(ks[1], (n_a, D, kva), sd * DN_BETA),
                              nrm(ks[2], (n_a, D, mq), sd)], axis=-1)
    w_in_b = jnp.concatenate([nrm(ks[3], (n_b, D, 2 * qb), sd),
                              nrm(ks[4], (n_b, D, vb), sd * DN_BETA),
                              nrm(ks[5], (n_b, D, mq), sd)], axis=-1)
    w_mem_kv = jnp.concatenate([nrm(ks[6], (DEPTH, D, mq), sd),
                                nrm(ks[7], (DEPTH, D, mq), sd * DN_BETA)], axis=-1)
    return {
        'x': nrm(ks[8], (BATCH, SEQ, D), 1.0),
        'mem': nrm(ks[9], (BATCH, MEM_LEN, D), 1.0),
        'w_in_a': w_in_a,
        'sinks': nrm(ks[10], (n_a, SWA_Q_HEADS), 0.5),
        'w_in_b': w_in_b,
        'lambda_qk': nrm(ks[11], (n_b, 4, HEAD_DIM), 0.1),
        'subln_g': 1.0 + nrm(ks[12], (n_b, DIFF_V_DIM), 0.02),
        'w_mem_kv': w_mem_kv,
        'w_out': nrm(ks[13], (DEPTH, D, D), sd * DN_BETA),
        'ln_g': 1.0 + nrm(ks[14], (DEPTH, 2, D), 0.02),
        'ln_b': nrm(ks[15], (DEPTH, 2, D), 0.02),
        'w_router': nrm(ks[16], (DEPTH, D, N_EXPERTS), sd),
        'router_bias': nrm(ks[17], (DEPTH, N_EXPERTS), 0.01),
        'w_gate': nrm(ks[18], (DEPTH, N_EXPERTS, D, EXPERT_HIDDEN), sd),
        'w_up': nrm(ks[19], (DEPTH, N_EXPERTS, D, EXPERT_HIDDEN), sd),
        'w_down': nrm(ks[20], (DEPTH, N_EXPERTS, EXPERT_HIDDEN, D), EXPERT_HIDDEN ** -0.5 * DN_BETA),
        'w_shared_gate': nrm(ks[21], (DEPTH, D, SHARED_HIDDEN), sd),
        'w_shared_up': nrm(ks[22], (DEPTH, D, SHARED_HIDDEN), sd),
        'w_shared_down': nrm(ks[23], (DEPTH, SHARED_HIDDEN, D), SHARED_HIDDEN ** -0.5 * DN_BETA),
    }

def reference(x, mem, w_in_a, sinks, w_in_b, lambda_qk, subln_g, w_mem_kv, w_out, ln_g, ln_b,
              w_router, router_bias, w_gate, w_up, w_down, w_shared_gate, w_shared_up, w_shared_down):
    B, S, D = x.shape
    slopes_a = alibi_slopes(SWA_Q_HEADS)
    slopes_b = alibi_slopes(DIFF_HEADS)
    qa, kva = SWA_Q_HEADS * HEAD_DIM, SWA_KV_HEADS * HEAD_DIM
    qb, vb = DIFF_HEADS * 2 * HEAD_DIM, DIFF_HEADS * DIFF_V_DIM
    for i in range(DEPTH):
        j = i // N_MIXERS
        if i % N_MIXERS == 0:
            h = x @ w_in_a[j]
            q, k, v, q_mem = jnp.split(h, [qa, qa + kva, qa + 2 * kva], axis=-1)
            mix = swa_sink_attention(q.reshape(B, S, SWA_Q_HEADS, HEAD_DIM),
                                     k.reshape(B, S, SWA_KV_HEADS, HEAD_DIM),
                                     v.reshape(B, S, SWA_KV_HEADS, HEAD_DIM),
                                     sinks[j], slopes_a)
        else:
            h = x @ w_in_b[j]
            q, k, v, q_mem = jnp.split(h, [qb, 2 * qb, 2 * qb + vb], axis=-1)
            lam_init = 0.8 - 0.6 * math.exp(-0.3 * i)
            lp = lambda_qk[j].astype(jnp.float32)
            lam = jnp.exp(jnp.sum(lp[0] * lp[1])) - jnp.exp(jnp.sum(lp[2] * lp[3])) + lam_init
            o = diff_attention(q.reshape(B, S, DIFF_HEADS, 2, HEAD_DIM),
                               k.reshape(B, S, DIFF_HEADS, 2, HEAD_DIM),
                               v.reshape(B, S, DIFF_HEADS, DIFF_V_DIM), lam, slopes_b)
            mix = (rms_norm(o, subln_g[j]) * (1.0 - lam_init)).reshape(B, S, vb)
        mem_out = memory_attention(q_mem.reshape(B, S, MEM_HEADS, HEAD_DIM), mem, w_mem_kv[i])
        y = jnp.concatenate([mix, mem_out], axis=-1) @ w_out[i]
        x = layer_norm(DN_ALPHA * x + y, ln_g[i, 0], ln_b[i, 0])
        f = moe_ffn(x, w_router[i], router_bias[i], w_gate[i], w_up[i], w_down[i],
                    w_shared_gate[i], w_shared_up[i], w_shared_down[i])
        x = layer_norm(DN_ALPHA * x + f, ln_g[i, 1], ln_b[i, 1])
    return x


_drawn_inputs = setup_inputs


def setup_inputs(seed=0):
    import zlib

    import numpy as np

    out = dict(_drawn_inputs(seed))
    spreads = {}
    factors = {'sinks': 2.99, 'subln_g': 3.894}
    for name, (base, spread) in spreads.items():
        noise = np.random.default_rng([zlib.crc32(name.encode()), seed]).standard_normal(out[name].shape)
        drawn = base * np.exp(spread * noise) if base else spread * noise
        out[name] = __import__('jax').numpy.asarray(drawn.astype(out[name].dtype))
    for name, factor in factors.items():
        out[name] = (out[name] * factor).astype(out[name].dtype)
    return out
```

```python
import math
from contextlib import ExitStack

import numpy as np

import concourse.bass as bass
from concourse import mybir

F32 = mybir.dt.float32
I32 = mybir.dt.int32
ALU = mybir.AluOpType
ACT = mybir.ActivationFunctionType
AX_X = mybir.AxisListType.X

P = 128
D = 1024
SEQ = 256
MEM = 256
HD = 64
DEPTH = 2
MEM_HEADS = 4
MIX_HEADS = D // HD - MEM_HEADS
KV_HEADS = MIX_HEADS // 4
DIFF_HEADS = MIX_HEADS // 2
NE = 64
NGROUP = 8
PER_GROUP = NE // NGROUP
TOPK_GROUPS = 4
HID = D // 4
ROUTED_SCALE = 2.5
ALPHA = (2.0 * DEPTH) ** 0.25
LN_EPS = 1e-5
SCALE = HD ** -0.5
WINDOW = 128

KT = D // P
TT = SEQ // P
FT = HID // P
SLOTS = 64
RING = 4
SLOT_F32 = 3 * KT * HID
PAIRS = NE // 2
UNROLL = RING // 2
STEPS = PAIRS // UNROLL
MASKED = -1.0e32
BIG = 1.0e30


def alibi_slopes(n):
    def pow2(m):
        start = 2.0 ** (-8.0 / m)
        return [start ** (i + 1) for i in range(m)]
    if n & (n - 1) == 0:
        s = pow2(n)
    else:
        c = 2 ** int(math.floor(math.log2(n)))
        s = pow2(c) + pow2(2 * c)[0::2][:n - c]
    return [float(v) for v in np.array(s, dtype=np.float32)]


def build_trunk(nc, x_in, mem_in, w_in_a, sinks, w_in_b, lambda_qk, subln_g, w_mem_kv, w_out, ln_g, ln_b,
                w_router, router_bias, w_gate, w_up, w_down, ws_gate, ws_up, ws_down, out):
    slopes = [alibi_slopes(MIX_HEADS), alibi_slopes(DIFF_HEADS)]
    lam_init = 0.8 - 0.6 * math.exp(-0.3 * 1)

    jobs = [
        [("mem", h, n, 0) for h in range(MEM_HEADS) for n in range(TT)]
        + [("self", h, n, 0) for h in range(MIX_HEADS) for n in range(TT)],
        [("mem", h, n, 0) for h in range(MEM_HEADS) for n in range(TT)]
        + [("self", h, n, c) for h in range(DIFF_HEADS) for n in range(TT) for c in range(2)],
    ]

    def keys_of(job):
        return MEM if job[0] == "mem" else (job[2] + 1) * P

    def has_product(layer, job):
        return layer == 0 or job[0] == "mem" or job[3] == 1

    products = [[j for j, job in enumerate(jobs[l]) if has_product(l, job)] for l in range(DEPTH)]

    plan = []
    for l in range(DEPTH):
        plan += [(l, "x", "DADA")] + [(l, "mem", "DADA")] * (l == 0) + [(l, "memkv", "DA")]
        plan += [(l, "q", "DAD"), (l, "k", "ADA"), (l, "v", "D" if l == 0 else "DADA"), (l, "qm", "A")]
        plan += [(l, "heads", "DAD")] * (l == 1)
        plan += [(l, "y", "DDDD"), (l, "xr", "DADA"), (l, "logit", "A"), (l, "hid", "AD"), (l, "rank", "D"), (l, "down", "DDDD")]
    G, readers = {}, ""
    for l, name, who in plan:
        G[l, name] = len(readers)
        readers += who

    items = [(0, "memkv"), (0, "in0"), (0, "in1"), (0, "out0"), (0, "out1"), (0, "shared"),
             (1, "memkv"), (1, "in0"), (1, "in1"), (1, "in2"), (1, "in3"), (1, "out0"), (1, "out1"), (1, "shared")]
    pre = [[it for it in items if it[0] == l] for l in range(DEPTH)]
    slot_of = {}
    for l in range(DEPTH):
        first = 0 if l == 0 else len(pre[0])
        for k, it in enumerate(pre[l]):
            slot_of[it] = (first + k) % RING
    expert_slot0 = [len(pre[0]) % RING, (len(pre[0]) + len(pre[1])) % RING]
    assert NE % RING == 0

    with ExitStack() as ctx:
        def sb(name, shape, dt=F32):
            return ctx.enter_context(nc.sbuf_tensor(name, shape, dt))

        named = {}

        def sem(name):
            if name not in named:
                named[name] = ctx.enter_context(nc.semaphore(name))
            return named[name]

        ring = sb("ring", [P, RING, SLOT_F32])
        x = sb("x", [P, TT, D])
        xT = sb("xT", [P, KT, SEQ])
        memT = sb("memT", [P, KT, MEM])
        acc = sb("acc", [P, TT, D])
        lnrow = sb("lnrow", [P, 2, 2, D])
        work = sb("work", [P, 9216])
        qT = work[:, 0:1536].rearrange("p (t n) -> p t n", n=SEQ)
        kT = work[:, 1536:3072].rearrange("p (t n) -> p t n", n=SEQ)
        v = work[:, 3072:4608].rearrange("p (t n) -> p t n", n=768)
        qmT = work[:, 4608:5120].rearrange("p (t n) -> p t n", n=SEQ)
        kmT = work[:, 5120:5632].rearrange("p (t n) -> p t n", n=MEM)
        vm = work[:, 5632:6144].rearrange("p (t n) -> p t n", n=MEM_HEADS * HD)
        mixT = work[:, 6144:8192].rearrange("p (t n) -> p t n", n=SEQ)
        heads = xT[:, 0:6, :].rearrange("p a b -> p (a b)").rearrange("p (t n) -> p t n", n=768)
        memnat = work[:, 0:2048].rearrange("p (t n) -> p t n", n=D)
        xg = [work[:, i * 1024:(i + 1) * 1024].rearrange("p (k s) -> p k s", k=KT) for i in range(2)]
        hidrow = work[:, 2048:2304]
        hT = work[:, 2304:2560].rearrange("p (f s) -> p f s", f=FT)
        sg = work[:, 2560:2816]
        y = work[:, 3072:4096]
        hot = [work[:, 4096 + i * 256:4352 + i * 256].rearrange("p (t s) -> p t s", t=TT) for i in range(2)]
        hotg = [work[:, 4608 + i * 256:4864 + i * 256].rearrange("p (t s) -> p t s", t=TT) for i in range(2)]
        back = [work[:, 5120 + i * 256:5376 + i * 256].rearrange("p (t n) -> p t n", t=TT) for i in range(2)]
        hsT = work[:, 8192:8704].rearrange("p (f n) -> p f n", f=FT)
        sgs = work[:, 8704:9216].rearrange("p (f n) -> p f n", f=FT)

        scratch = acc[:].rearrange("p t n -> p (t n)")
        score = [scratch[:, i * 256:(i + 1) * 256] for i in range(3)]
        prob = [scratch[:, 768 + i * 256:1024 + i * 256] for i in range(3)]
        soft = [sb(f"soft{i}", [P, 256]) for i in range(3)]
        softT = [sb(f"softT{i}", [P, 2, P]) for i in range(2)]
        rowmax = sb("rowmax", [P, 32])
        negmax = sb("negmax", [P, 32])
        rowsum = sb("rowsum", [P, 32])
        sinkexp = sb("sinkexp", [P, 32])
        rden = sb("rden", [P, 32])

        ident = sb("ident", [P, P])
        ones = sb("ones", [P, P])
        before = sb("before", [P, P])
        negdist = [sb(f"negdist{l}", [P, 2 * P]) for l in range(DEPTH)]
        iota0 = sb("iota0", [P, SLOTS])
        slot_no = sb("slot_no", [P, SLOTS])
        lower = sb("lower", [P, NGROUP, NGROUP])
        sinkrow = sb("sinkrow", [P, MIX_HEADS])
        biasrow = sb("biasrow", [P, DEPTH, NE])
        lamrow = sb("lamrow", [P, 4, HD])
        sublnrow = sb("sublnrow", [P, 2 * HD])
        lamv = sb("lamv", [P, 8])
        lamp = sb("lamp", [P, 2, HD])
        eps = sb("eps", [P, 1])
        stats = sb("stats", [P, TT, 2, 6])
        mv = sb("mv", [P, TT, 2])
        std = sb("std", [P, TT, 1])
        rstd = sb("rstd", [P, TT, 1])
        hsq = sb("hsq", [P, 12])
        hstd = sb("hstd", [P, 12])
        hrstd = sb("hrstd", [P, 12])
        wr = sb("wr", [P, DEPTH, KT, NE])
        rsc = sb("rsc", [P, TT, NE])
        aff = sb("aff", [P, TT, NE])
        sel = sb("sel", [P, TT, NE])
        top2 = sb("top2", [P, TT, NGROUP, 8])
        gsc = sb("gsc", [P, TT, NGROUP])
        cmp1 = sb("cmp1", [P, TT, NGROUP, NGROUP])
        cmp2 = sb("cmp2", [P, TT, NGROUP, NGROUP])
        grank = sb("grank", [P, TT, NGROUP])
        gmask = sb("gmask", [P, TT, NGROUP])
        goff = sb("goff", [P, TT, NGROUP])
        top8 = sb("top8", [P, TT, 8])
        chosen = sb("chosen", [P, TT, NE])
        gate = sb("gate", [P, TT, NE])
        gsum = sb("gsum", [P, TT])
        grec = sb("grec", [P, TT])
        rank = sb("rank", [P, TT, NE])
        cmax = sb("cmax", [P, 1])
        more = sb("more", [P, 3])
        nround = sb("nround", [P, 1])
        nround_i = sb("nround_i", [P, DEPTH], I32)

        banks = [ctx.enter_context(nc.psum_tensor(f"bank{i}", [P, 512], F32)) for i in range(8)]

        def by_row_run(w):
            return w.rearrange("(p k) n -> p k n", k=KT)

        def item_loads(it):
            l, name = it
            s = ring[:, slot_of[it], :]
            if name == "memkv":
                return [(s[:, 0:KT * 512].rearrange("p (k n) -> p k n", k=KT), by_row_run(w_mem_kv[l]))]
            if name == "shared":
                return expert_loads(s, ws_gate[l], ws_up[l], ws_down[l])
            if name[:3] == "out":
                half = int(name[3])
                src = w_out[l].rearrange("(k p) n -> p k n", p=P)[:, :, half * 512:half * 512 + 512]
                return [(s[:, 0:KT * 512].rearrange("p (k n) -> p k n", k=KT), src)]
            w = by_row_run((w_in_a if l == 0 else w_in_b)[0])
            c0 = int(name[2]) * 768
            n = min(768, w.shape[2] - c0)
            return [(s[:, 0:KT * n].rearrange("p (k n) -> p k n", k=KT), w[:, :, c0:c0 + n])]

        def expert_loads(s, g, u, dn):
            n = KT * HID
            return [(s[:, 0:n].rearrange("p (k n) -> p k n", k=KT), by_row_run(g)),
                    (s[:, n:2 * n].rearrange("p (k n) -> p k n", k=KT), by_row_run(u)),
                    (s[:, 2 * n:3 * n].rearrange("p (f n) -> p f n", f=FT), dn.rearrange("(p f) n -> p f n", f=FT))]

        def item_view(it, n):
            return ring[:, slot_of[it], 0:KT * n].rearrange("p (k n) -> p k n", k=KT)

        def expert_view(slot):
            n = KT * HID
            s = ring[:, slot, :]
            return (s[:, 0:2 * n].rearrange("p (j k f) -> p k j f", j=2, k=KT),
                    s[:, 2 * n:3 * n].rearrange("p (f n) -> p f n", f=FT))

        def last_group(it):
            l, name = it
            phase, n = {"memkv": ("memkv", 1), "in0": ("q", 2), "in1": ("qm", 0) if l == 0 else ("k", 2), "in2": ("v", 3),
                        "in3": ("qm", 0), "out0": ("y", 1), "out1": ("y", 3), "shared": ("down", 3)}[name]
            return G[l, phase] + n

        def landed(eng, it):
            eng.wait_ge(sem(f"landed_{it[1]}_{it[0]}"), 16 * len(item_loads(it)))

        def evacuated(eng, g):
            eng.wait_ge(sem("read_by_" + readers[g]), readers[:g + 1].count(readers[g]))

        def bank_free(pe, g):
            if g >= 4:
                evacuated(pe, g - 4)

        def filled(eng, g):
            eng.wait_ge(sem("group"), g + 1)

        def bank_of(g, n, width):
            return banks[g % 4][:, 0:n * width].rearrange("p (a b) -> p a b", a=n)

        block = ctx.enter_context(nc.Block())

        CONSTS = 13
        ROWS = 4 + DEPTH

        @block.sync
        def _(sp):
            sp.dma_start(x[:], x_in[0].rearrange("(t p) d -> p t d", p=P)).then_inc(sem("x_in"), 16)

            def load(it):
                for dst, src in item_loads(it):
                    sp.dma_start(dst, src).then_inc(sem(f"landed_{it[1]}_{it[0]}"), 16)

            def experts(l, i, k):
                slot = (expert_slot0[l] + k) % RING
                e = RING * i + k
                srcs = [w[l, bass.ds(e, 1)].rearrange("a r n -> (a r) n") for w in (w_gate, w_up, w_down)]
                for dst, src in expert_loads(ring[:, slot, :], *srcs):
                    sp.dma_start(dst, src).then_inc(sem(f"expert_landed{k}_{l}"), 16)

            def reload(l, done, i, k):
                sp.wait_ge(sem(f"down_done_{l}"), done)
                experts(l, i, k)

            extra = None
            for l in range(DEPTH):
                for k, it in enumerate(pre[l]):
                    if k >= RING:
                        filled(sp, last_group(pre[l][k - RING]))
                    elif l > 0:
                        sp.wait_ge(sem(f"down_done_{l - 1}"), extra * NE + (NE - RING + 2 * (k // 2) + 2))
                    load(it)
                for k in range(RING):
                    filled(sp, last_group(pre[l][len(pre[l]) - RING + k]))
                    experts(l, 0, k)
                with sp.Fori(0, STEPS - 1) as i:
                    for k in range(RING):
                        reload(l, RING * i + (2 * (k // 2) + 2), i + 1, k)
                sp.wait_ge(sem(f"routed_{l}"), 1)
                extra = sp.snap(sp.value_load(nround_i[0:1, l:l + 1], min_val=0, max_val=3))
                with sp.If(extra > 0):
                    with sp.Fori(0, extra) as r:
                        with sp.Fori(0, STEPS) as i:
                            for k in range(RING):
                                reload(l, r * NE + RING * i + (NE - RING + 2 * (k // 2) + 2), i, k)
            sp.wait_ge(sem("normed"), 2 * DEPTH)
            sp.dma_start(out[0].rearrange("(t p) d -> p t d", p=P), x[:]).then_inc(sem("out"), 16)
            sp.wait_ge(sem("out"), 16)

        @block.gpsimd
        def _(pool):
            made = sem("const")
            n = 0

            def step(ins):
                nonlocal n
                n += 1
                ins.then_inc(made, 1)
                pool.wait_ge(made, n)

            pool.dma_start(lamrow[:], lambda_qk[0].rearrange("(o a) b -> o a b", o=1).broadcast_to([P, 4, HD])).then_inc(sem("rows"), 16)
            pool.dma_start(sublnrow[:], subln_g.broadcast_to([P, 2 * HD])).then_inc(sem("rows"), 16)
            pool.dma_start(sinkrow[:], sinks.broadcast_to([P, MIX_HEADS])).then_inc(sem("rows"), 16)
            pool.dma_start(biasrow[:], router_bias.rearrange("(o a) b -> o a b", o=1).broadcast_to([P, DEPTH, NE])).then_inc(sem("rows"), 16)
            for l in range(DEPTH):
                pool.dma_start(wr[:, l], by_row_run(w_router[l])).then_inc(sem("rows"), 16)
            step(pool.memset(ident[:], 0.0))
            step(pool.affine_select(out=ident[:], in_=ident[:], compare_op=ALU.not_equal, fill=1.0, base=0,
                                    pattern=[[-1, P]], channel_multiplier=1))
            step(pool.memset(ones[:], 1.0))
            step(pool.affine_select(out=before[:], in_=ones[:], compare_op=ALU.is_gt, fill=0.0, base=0,
                                    pattern=[[1, P]], channel_multiplier=-1))
            for l in range(DEPTH):
                nd = negdist[l]
                step(pool.iota(nd[:], pattern=[[1, 2 * P]], base=-P, channel_multiplier=-1,
                               allow_small_or_imprecise_dtypes=True))
                step(pool.affine_select(out=nd[:], in_=nd[:], compare_op=ALU.is_ge, fill=MASKED, base=P,
                                        pattern=[[-1, 2 * P]], channel_multiplier=1))
                if l == 0:
                    step(pool.affine_select(out=nd[:], in_=nd[:], compare_op=ALU.is_ge, fill=MASKED,
                                            base=WINDOW - 1 - P, pattern=[[1, 2 * P]], channel_multiplier=-1))
            step(pool.iota(iota0[:], pattern=[[1, SLOTS]], base=0, channel_multiplier=0,
                           allow_small_or_imprecise_dtypes=True))
            step(pool.memset(lower[:], 1.0))
            step(pool.affine_select(out=lower[:], in_=lower[:], compare_op=ALU.is_gt, fill=0.0, base=0,
                                    pattern=[[1, NGROUP], [-1, NGROUP]], channel_multiplier=0))
            step(pool.memset(eps[:], LN_EPS))
            assert n == CONSTS

        @block.tensor
        def _(pe):
            pe.wait_ge(sem("const"), CONSTS)

            def transposes(src, g0):
                for n in range(4):
                    t, half = n // 2, n % 2
                    bank_free(pe, g0 + n)
                    for k in range(4):
                        last = pe.transpose(banks[(g0 + n) % 4][:, k * P:(k + 1) * P],
                                            src[:, t, 4 * half + k:D:KT], ident[:])
                    last.then_inc(sem("group"), 1)

            def product(dst, pairs):
                for n, (a, b) in enumerate(pairs):
                    last = pe.matmul(dst, a, b, start=(n == 0), stop=(n == len(pairs) - 1))
                return last

            def chunks(w, c0, m, moving):
                return [(w[:, k, c0:c0 + m], moving[:, k, :]) for k in range(KT)]

            def rows(stationary, t, w, c0, n):
                return [(stationary[:, k, t * P:(t + 1) * P], w[:, k, c0:c0 + n]) for k in range(KT)]

            for l in range(DEPTH):
                if l == 0:
                    pe.wait_ge(sem("x_in"), 16)
                else:
                    pe.wait_ge(sem("normed"), 2 * l)
                transposes(x, G[l, "x"])
                if l == 0:
                    pe.wait_ge(sem("mem_in"), 16)
                    transposes(memnat, G[l, "mem"])
                    for g in range(G[l, "mem"], G[l, "mem"] + 4):
                        evacuated(pe, g)

                g = G[l, "memkv"]
                landed(pe, (l, "memkv"))
                w = item_view((l, "memkv"), 512)
                bank_free(pe, g)
                for c in range(2):
                    last = product(banks[g % 4][:, c * 256:(c + 1) * 256], chunks(w, c * P, P, memT))
                last.then_inc(sem("group"), 1)
                bank_free(pe, g + 1)
                for t in range(2):
                    last = product(banks[(g + 1) % 4][:, t * 256:(t + 1) * 256], rows(memT, t, w, 256, 256))
                last.then_inc(sem("group"), 1)
                for n in range(4):
                    evacuated(pe, G[l, "x"] + n)

                def tile_pair(g, w, c0):
                    bank_free(pe, g)
                    for c in range(2):
                        last = product(banks[g % 4][:, c * 256:(c + 1) * 256], chunks(w, c0 + c * P, P, xT))
                    last.then_inc(sem("group"), 1)

                landed(pe, (l, "in0"))
                for n in range(3):
                    tile_pair(G[l, "q"] + n, item_view((l, "in0"), 768), n * 2 * P)
                landed(pe, (l, "in1"))
                if l == 0:
                    w = item_view((0, "in1"), 640)
                    for n in range(KV_HEADS):
                        g = G[0, "k"] + n
                        bank_free(pe, g)
                        product(banks[g % 4][0:HD, 0:SEQ], chunks(w, n * HD, HD, xT)).then_inc(sem("group"), 1)
                    g = G[0, "v"]
                    bank_free(pe, g)
                    for t in range(TT):
                        last = product(banks[g % 4][:, t * 192:(t + 1) * 192], rows(xT, t, w, 192, 192))
                    last.then_inc(sem("group"), 1)
                    wm = w[:, :, 384:640]
                else:
                    for n in range(3):
                        tile_pair(G[1, "k"] + n, item_view((1, "in1"), 768), n * 2 * P)
                    landed(pe, (1, "in2"))
                    w = item_view((1, "in2"), 768)
                    for n in range(4):
                        g = G[1, "v"] + n
                        bank_free(pe, g)
                        last = product(banks[g % 4][:, 0:384], rows(xT, n // 2, w, n % 2 * 384, 384))
                        last.then_inc(sem("group"), 1)
                    landed(pe, (1, "in3"))
                    wm = item_view((1, "in3"), 256)
                tile_pair(G[l, "qm"], wm, 0)
                for g in range(G[l, "memkv"], G[l, "qm"] + 1):
                    evacuated(pe, g)

                J = len(jobs[l])
                base = 0 if l == 0 else len(jobs[0])
                pbase = 0 if l == 0 else len(products[0])

                def scores(j):
                    kind, h, n, c = jobs[l][j]
                    s = base + j
                    if s >= 2:
                        pe.wait_ge(sem("score_read"), s - 1)
                    if kind == "mem":
                        lo, tile, ktile, q, kk = (h % 2) * HD, h // 2, h // 2, qmT, kmT
                    elif l == 0:
                        lo, tile, ktile, q, kk = (h % 2) * HD, h // 2, h // 4, qT, kT
                    else:
                        lo, tile, ktile, q, kk = c * HD, h, h, qT, kT
                    pe.matmul(banks[4 + s % 2][:, 0:keys_of(jobs[l][j])], q[lo:lo + HD, tile, n * P:(n + 1) * P],
                              kk[lo:lo + HD, ktile, 0:keys_of(jobs[l][j])], start=True, stop=True)\
                        .then_inc(sem("scored"), 1)

                def turn(j):
                    if j not in products[l]:
                        return
                    s, m = base + j, pbase + products[l].index(j)
                    pe.wait_ge(sem("softened"), s + 1)
                    if m >= 2:
                        pe.wait_ge(sem("turned"), m - 1)
                    for t in range(keys_of(jobs[l][j]) // P):
                        last = pe.transpose(banks[6 + m % 2][:, t * P:(t + 1) * P], soft[s % 3][:, t * P:(t + 1) * P], ident[:])
                    last.then_inc(sem("turning"), 1)

                def values(j):
                    if j not in products[l]:
                        return
                    kind, h, n, c = jobs[l][j]
                    m = pbase + products[l].index(j)
                    pe.wait_ge(sem("turned"), m + 1)
                    if m >= 2:
                        pe.wait_ge(sem("headed"), m - 1)
                    bank = banks[2 + m % 2]
                    nt = keys_of(jobs[l][j]) // P
                    if kind == "mem" or l == 0:
                        lo = (h % 2) * HD
                        col = h * HD if kind == "mem" else (h // 4) * HD
                        vv = vm if kind == "mem" else v
                        last = product(bank[lo:lo + HD, 0:P], [(vv[:, t, col:col + HD], softT[m % 2][:, t, :]) for t in range(nt)])
                    else:
                        last = product(bank[:, 0:P], [(softT[m % 2][:, t, :], v[:, t, h * P:(h + 1) * P]) for t in range(nt)])
                    last.then_inc(sem("valued"), 1)

                for j in range(J + 3):
                    if j < J:
                        scores(j)
                    if 2 <= j < J + 2:
                        turn(j - 2)
                    if j >= 3:
                        values(j - 3)
                pe.wait_ge(sem("headed"), pbase + len(products[l]))

                if l == 1:
                    pe.wait_ge(sem("heads_normed"), 1)
                    g = G[l, "heads"]
                    for n in range(3):
                        bank_free(pe, g + n)
                        for c in range(4):
                            h, t = (4 * n + c) // 2, c % 2
                            last = pe.transpose(banks[(g + n) % 4][:, c * P:(c + 1) * P], heads[:, t, h * P:(h + 1) * P], ident[:])
                        last.then_inc(sem("group"), 1)
                    for n in range(3):
                        evacuated(pe, g + n)

                g = G[l, "y"]
                for half in range(2):
                    it = (l, f"out{half}")
                    landed(pe, it)
                    w = item_view(it, 512)
                    for t in range(TT):
                        bank_free(pe, g + 2 * half + t)
                        last = product(banks[(g + 2 * half + t) % 4][:], rows(mixT, t, w, 0, 512))
                        last.then_inc(sem("group"), 1)

                pe.wait_ge(sem("normed"), 2 * l + 1)
                transposes(x, G[l, "xr"])
                for n in range(4):
                    evacuated(pe, G[l, "xr"] + n)
                g = G[l, "logit"]
                bank_free(pe, g)
                for t in range(TT):
                    last = product(banks[g % 4][:, t * NE:(t + 1) * NE], rows(xT, t, wr[:, l], 0, NE))
                last.then_inc(sem("group"), 1)

                g2 = G[l, "hid"]
                it = (l, "shared")
                landed(pe, it)
                wgu, wd = expert_view(slot_of[it])
                for n in range(2):
                    bank_free(pe, g2 + n)
                    for f in range(FT):
                        last = product(banks[(g2 + n) % 4][:, f * SEQ:(f + 1) * SEQ],
                                       [(wgu[:, k, n, f:HID:FT], xT[:, k, :]) for k in range(KT)])
                    last.then_inc(sem("group"), 1)

                pe.wait_ge(sem("chosen"), l + 1)
                g = G[l, "rank"]
                bank_free(pe, g)
                bank = banks[g % 4]
                product(bank[:, 0:NE], [(before[:], chosen[:, 0, :])])
                product(bank[:, NE:2 * NE], [(ones[:], chosen[:, 0, :]), (before[:], chosen[:, 1, :])])
                product(bank[:, 2 * NE:3 * NE], [(ones[:], chosen[:, 0, :]), (ones[:], chosen[:, 1, :])])\
                    .then_inc(sem("group"), 1)

                g = G[l, "down"]
                evacuated(pe, G[l, "hid"] + 1)
                pe.wait_ge(sem("routed_" + str(l)), 1)
                for n in range(4):
                    t, half = n // 2, n % 2
                    bank_free(pe, g + n)
                    last = product(banks[(g + n) % 4][:], [(hsT[:, f, t * P:(t + 1) * P], wd[:, f, half * 512:half * 512 + 512])
                                                           for f in range(FT)])
                    last.then_inc(sem("group"), 1)
                for n in range(4):
                    evacuated(pe, g + n)

                def s_(name):
                    return sem(f"{name}_{l}")

                def front(U, b):
                    pe.wait_ge(s_("hot_ready"), U + 1)
                    pe.wait_ge(s_("xg_act"), U + 1)
                    pe.wait_ge(s_("xg_dve"), U + 1)
                    for k in range(KT):
                        last = product(banks[k // 4][:, (k % 4) * P:(k % 4 + 1) * P],
                                       [(x[:, t, k:D:KT], hot[b][:, t, :]) for t in range(TT)])
                        if k % 4 == 3:
                            last.then_inc(s_("gathered"), 1)
                    pe.wait_ge(s_("back_ready"), U + 1)
                    pe.wait_ge(s_("hT_ready"), U + 1)
                    for t in range(TT):
                        last = pe.transpose(banks[3][:, 256 + t * P:256 + (t + 1) * P], hotg[b][:, t, :], ident[:])
                    last.then_inc(s_("hot_used"), 1)

                def slots_of(e):
                    return slice(e * SLOTS, (e + 1) * SLOTS)

                def gate_up(U, b, rs):
                    for e in range(2):
                        pe.wait_ge(s_(f"expert_landed{2 * b + e}"), rs * 48 + 48)
                    pe.wait_ge(s_("xg_act"), U + 2)
                    pe.wait_ge(s_("xg_dve"), U + 2)
                    w = [expert_view((expert_slot0[l] + 2 * b + e) % RING)[0] for e in range(2)]
                    for k in range(KT):
                        for e in range(2):
                            last = pe.matmul(banks[2][slots_of(e), :], xg[b][:, k, slots_of(e)], w[e][:, k],
                                             start=(k == 0), stop=(k == KT - 1))
                    last.then_inc(s_("hidden"), 1)

                def turn_h(U):
                    pe.wait_ge(s_("h_ready"), U + 1)
                    for f in range(FT):
                        last = pe.transpose(banks[3][:, f * P:(f + 1) * P], hidrow[:, f:HID:FT], ident[:])
                    last.then_inc(s_("h_turned"), 1)

                def down(U, b):
                    pe.wait_ge(s_("hT_ready"), U + 2)
                    w = [expert_view((expert_slot0[l] + 2 * b + e) % RING)[1] for e in range(2)]
                    for half in range(2):
                        for f in range(FT):
                            for e in range(2):
                                last = pe.matmul(banks[4 + half][slots_of(e), :], hT[:, f, slots_of(e)],
                                                 w[e][:, f, half * 512:half * 512 + 512], start=(f == 0), stop=(f == FT - 1))
                        last.then_inc(s_("down_done"), 1)

                def scatter(U, b):
                    pe.wait_ge(s_("y_act"), U + 1)
                    pe.wait_ge(s_("y_dve"), U + 1)
                    for q in range(4):
                        t, half = q // 2, q % 2
                        pe.wait_ge(s_("added"), 4 * U + q + 3)
                        pe.matmul(banks[6 + q % 2][:], back[b][:, t, :], y[:, half * 512:half * 512 + 512],
                                  start=True, stop=True).then_inc(s_("scattered"), 1)

                def unit(r, i, b, first=False, last=False):
                    U = r * PAIRS + UNROLL * i + b
                    rs = r * STEPS + i
                    gate_up(U, b, rs)
                    if not first:
                        scatter(U - 1, 1 - b)
                    turn_h(U)
                    if not last:
                        front(U + 1, 1 - b)
                    down(U, b)

                rounds = pe.value_load(nround_i[0:1, l:l + 1], min_val=0, max_val=3) + 1
                with pe.Fori(0, rounds) as r:
                    front(r * PAIRS, 0)
                    unit(r, 0, 0, first=True)
                    unit(r, 0, 1)
                    with pe.Fori(1, STEPS - 1) as i:
                        unit(r, i, 0)
                        unit(r, i, 1)
                    unit(r, STEPS - 1, 0)
                    unit(r, STEPS - 1, 1, last=True)
                    scatter(r * PAIRS + PAIRS - 1, 1)

        def evacuate(eng, me, l, copy, scaled):
            def share(name):
                for n in range(len(readers)):
                    g = G[l, name] + n
                    if (l, name, readers[G[l, name]:g + 1]) not in begun:
                        return
                    if readers[g] == me:
                        filled(eng, g)
                        yield n, g

            begun = {(l_, name, who[:n + 1]) for l_, name, who in plan for n in range(len(who))}
            done = sem("read_by_" + me)
            for name, dst in [("x", xT)] + [("mem", memT)] * (l == 0):
                for n, g in share(name):
                    t, half = n // 2, n % 2
                    copy(dst[:, 4 * half:4 * half + 4, t * P:(t + 1) * P], bank_of(g, 4, P)).then_inc(done, 1)
            for n, g in share("memkv"):
                copy((kmT, vm)[n], bank_of(g, 2, 256)).then_inc(done, 1)
            for n, g in share("q"):
                scaled(qT[:, 2 * n:2 * n + 2, :], bank_of(g, 2, SEQ)).then_inc(done, 1)
            for n, g in share("k"):
                if l == 0:
                    copy(kT[0:HD, n, :], banks[g % 4][0:HD, 0:SEQ])
                    copy(kT[HD:2 * HD, n, :], banks[g % 4][0:HD, 0:SEQ]).then_inc(done, 1)
                else:
                    copy(kT[:, 2 * n:2 * n + 2, :], bank_of(g, 2, SEQ)).then_inc(done, 1)
            for n, g in share("v"):
                if l == 0:
                    copy(v[:, :, 0:192], bank_of(g, 2, 192)).then_inc(done, 1)
                else:
                    copy(v[:, n // 2, n % 2 * 384:n % 2 * 384 + 384], banks[g % 4][:, 0:384]).then_inc(done, 1)
            for n, g in share("qm"):
                scaled(qmT, bank_of(g, 2, SEQ)).then_inc(done, 1)

        @block.scalar
        def _(act):
            read = sem("read_by_A")
            act.dma_start(memnat, mem_in[0].rearrange("(t p) d -> p t d", p=P)).then_inc(sem("mem_in"), 16)

            def load_norm(n):
                for i, w in enumerate((ln_g, ln_b)):
                    act.dma_start(lnrow[:, n % 2, i, :], w[n // 2, n % 2:n % 2 + 1, :].broadcast_to([P, D]))\
                       .then_inc(sem(f"lnrow{n}"), 16)

            def norm_std(n):
                act.wait_ge(sem("stats"), n + 1)
                for t in range(TT):
                    last = act.activation(std[:, t, :], mv[:, t, 1:2], ACT.Sqrt, bias=eps[:])
                last.then_inc(sem("std"), 1)

            def copy(dst, src):
                return act.activation(dst, src, ACT.Copy)

            def scaled(dst, src):
                return act.activation(dst, src, ACT.Copy, scale=SCALE)

            load_norm(0)
            load_norm(1)
            act.wait_ge(sem("const"), CONSTS)
            act.wait_ge(sem("rows"), ROWS * 16)
            act.wait_ge(sem("lam_sum"), 1)
            act.activation(lamv[:, 2:4], lamv[:, 0:2], ACT.Exp).then_inc(sem("lam_exp"), 1)

            for l in range(DEPTH):
                evacuate(act, "A", l, copy, scaled)

                base = 0 if l == 0 else len(jobs[0])
                pbase = 0 if l == 0 else len(products[0])
                J = len(jobs[l])

                def exps(j):
                    s = base + j
                    w = keys_of(jobs[l][j])
                    act.wait_ge(sem("biased"), s + 1)
                    if s >= 3:
                        act.wait_ge(sem("softened"), s - 2)
                    last = act.activation(prob[s % 3][:, 0:w], score[s % 3][:, 0:w], ACT.Exp, bias=negmax[:, j:j + 1],
                                          accum_out=rowsum[:, j:j + 1])
                    if l == 0 and jobs[l][j][0] == "self":
                        h = jobs[l][j][1]
                        last = act.activation(sinkexp[:, j:j + 1], sinkrow[:, h:h + 1], ACT.Exp, bias=negmax[:, j:j + 1])
                    last.then_inc(sem("exped"), 1)

                def turned(j):
                    if j not in products[l]:
                        return
                    m = pbase + products[l].index(j)
                    nt = keys_of(jobs[l][j]) // P
                    act.wait_ge(sem("turning"), m + 1)
                    if m >= 2:
                        act.wait_ge(sem("valued"), m - 1)
                    copy(softT[m % 2][:, 0:nt, :], banks[6 + m % 2][:, 0:nt * P].rearrange("p (t n) -> p t n", n=P))\
                        .then_inc(sem("turned"), 1)

                for j in range(J + 2):
                    if j < J:
                        exps(j)
                    if j >= 2:
                        turned(j - 2)

                if l == 1:
                    act.wait_ge(sem("head_sq"), 1)
                    act.activation(hstd[:], hsq[:], ACT.Sqrt, bias=eps[:], scale=1.0 / (2 * HD)).then_inc(sem("head_std"), 1)
                    g = G[l, "heads"] + 1
                    filled(act, g)
                    copy(mixT[:, 2:4, :], bank_of(g, 2, SEQ)).then_inc(read, 1)
                norm_std(2 * l)
                if l == 0:
                    act.wait_ge(sem("normed"), 1)
                    load_norm(2)
                for n in (1, 3):
                    g = G[l, "xr"] + n
                    filled(act, g)
                    copy(xT[:, 4:8, n // 2 * P:(n // 2 + 1) * P], bank_of(g, 4, P)).then_inc(read, 1)
                g = G[l, "logit"]
                filled(act, g)
                act.activation(rsc[:], bank_of(g, TT, NE), ACT.Exp, scale=-1.0).then_inc(read, 1)
                g = G[l, "hid"]
                filled(act, g)
                act.activation(sgs, bank_of(g, FT, SEQ), ACT.Silu).then_inc(read, 1)

                def s_(name):
                    return sem(f"{name}_{l}")

                def silu(U):
                    act.wait_ge(s_("hidden"), U + 1)
                    act.activation(sg, banks[2][:, 0:HID], ACT.Silu).then_inc(s_("silu"), 1)

                def hT_out(U):
                    act.wait_ge(s_("h_turned"), U + 1)
                    copy(hT, banks[3][:, 0:FT * P].rearrange("p (f s) -> p f s", f=FT)).then_inc(s_("hT_ready"), 1)

                def y_out(U):
                    act.wait_ge(s_("down_done"), 2 * U + 1)
                    copy(y[:, 0:512], banks[4][:]).then_inc(s_("y_act"), 1)

                def gathered(U, b):
                    act.wait_ge(s_("gathered"), 2 * U + 1)
                    copy(xg[b][:, 0:4, :], banks[0][:].rearrange("p (k s) -> p k s", k=4)).then_inc(s_("xg_act"), 1)
                    act.wait_ge(s_("hot_used"), U + 3)
                    copy(back[b], banks[3][:, 256:256 + TT * P].rearrange("p (t n) -> p t n", t=TT)).then_inc(s_("back_ready"), 1)

                def unit(r, i, b, first=False, last=False):
                    U = r * PAIRS + i * UNROLL + b
                    silu(U)
                    hT_out(U)
                    if not last:
                        gathered(U + 1, 1 - b)
                    y_out(U)

                act.sem_inc(s_("xg_act"), 1)
                act.sem_inc(s_("back_ready"), 1)
                act.sem_inc(s_("hT_ready"), 1)
                act.wait_ge(s_("routed"), 1)
                rounds = act.value_load(nround_i[0:1, l:l + 1], min_val=0, max_val=3) + 1
                with act.Fori(0, rounds) as r:
                    gathered(r * PAIRS, 0)
                    unit(r, 0, 0, first=True)
                    unit(r, 0, 1)
                    with act.Fori(1, STEPS - 1) as i:
                        unit(r, i, 0)
                        unit(r, i, 1)
                    unit(r, STEPS - 1, 0)
                    unit(r, STEPS - 1, 1, last=True)
                norm_std(2 * l + 1)
                if l == 0:
                    act.wait_ge(sem("normed"), 2)
                    load_norm(3)

        @block.vector
        def _(dve):
            read = sem("read_by_D")
            link_count = 0

            def link(ins):
                nonlocal link_count
                link_count += 1
                ins.then_inc(sem("dve_link"), 1)
                dve.wait_ge(sem("dve_link"), link_count)

            def copy(dst, src):
                return dve.tensor_copy(dst, src)

            def scaled(dst, src):
                return dve.tensor_scalar(dst, src, SCALE, None, ALU.mult)

            def norm(n, src):
                for t in range(TT):
                    for half in range(2):
                        last = dve.bn_stats(stats[:, t, half, :], src[:, t, half * 512:half * 512 + 512])
                link(last)
                for t in range(TT):
                    last = dve.bn_aggr(mv[:, t, :], stats[:, t, :, :])
                last.then_inc(sem("stats"), 1)
                dve.wait_ge(sem("std"), n + 1)
                link(dve.reciprocal(rstd[:], std[:]))
                dve.wait_ge(sem(f"lnrow{n}"), 32)
                for t in range(TT):
                    last = dve.tensor_scalar(x[:, t, :], src[:, t, :], mv[:, t, 0:1], rstd[:, t, :], ALU.subtract, ALU.mult)
                link(last)
                for t in range(TT):
                    last = dve.tensor_tensor(x[:, t, :], x[:, t, :], lnrow[:, n % 2, 0, :], ALU.mult)
                link(last)
                for t in range(TT):
                    last = dve.tensor_tensor(x[:, t, :], x[:, t, :], lnrow[:, n % 2, 1, :], ALU.add)
                last.then_inc(sem("normed"), 1)

            dve.wait_ge(sem("const"), CONSTS)
            dve.wait_ge(sem("rows"), ROWS * 16)
            link(dve.tensor_tensor(lamp[:], lamrow[:, 0:4:2, :], lamrow[:, 1:4:2, :], ALU.mult))
            dve.tensor_reduce(lamv[:, 0:2], lamp[:], AX_X, ALU.add).then_inc(sem("lam_sum"), 1)
            dve.wait_ge(sem("lam_exp"), 1)
            dve.scalar_tensor_tensor(out=lamv[:, 4:5], in0=lamv[:, 3:4], scalar=-lam_init, in1=lamv[:, 2:3],
                                     op0=ALU.add, op1=ALU.subtract)
            link(dve.tensor_scalar(sublnrow[:], sublnrow[:], 1.0 - lam_init, None, ALU.mult))

            for l in range(DEPTH):
                evacuate(dve, "D", l, copy, scaled)

                base = 0 if l == 0 else len(jobs[0])
                pbase = 0 if l == 0 else len(products[0])
                J = len(jobs[l])

                def bias(j):
                    kind, h, n, c = jobs[l][j]
                    s, w = base + j, keys_of(jobs[l][j])
                    dve.wait_ge(sem("scored"), s + 1)
                    if s >= 3:
                        dve.wait_ge(sem("exped"), s - 2)
                    src, dst = banks[4 + s % 2][:, 0:w], score[s % 3][:, 0:w]
                    if kind == "mem":
                        copy(dst, src).then_inc(sem("score_read"), 1)
                    else:
                        dve.scalar_tensor_tensor(out=dst, in0=negdist[l][:, (1 - n) * P:2 * P], scalar=slopes[l][h], in1=src,
                                                 op0=ALU.mult, op1=ALU.add).then_inc(sem("score_read"), 1)
                    dve.wait_ge(sem("score_read"), s + 1)
                    link(dve.tensor_reduce(rowmax[:, j:j + 1], dst, AX_X, ALU.max))
                    if kind == "self" and l == 0:
                        last = dve.tensor_scalar(negmax[:, j:j + 1], rowmax[:, j:j + 1], sinkrow[:, h:h + 1], -1.0, ALU.max, ALU.mult)
                    else:
                        last = dve.tensor_scalar(negmax[:, j:j + 1], rowmax[:, j:j + 1], -1.0, None, ALU.mult)
                    last.then_inc(sem("biased"), 1)

                def soften(j):
                    kind, h, n, c = jobs[l][j]
                    s, w = base + j, keys_of(jobs[l][j])
                    col = slice(j, j + 1)
                    dve.wait_ge(sem("exped"), s + 1)
                    if kind == "self" and l == 0:
                        link(dve.tensor_tensor(rowsum[:, col], rowsum[:, col], sinkexp[:, col], ALU.add))
                    link(dve.reciprocal(rden[:, col], rowsum[:, col]))
                    if s >= 3 and (j >= 3 or l > 0):
                        old = j - 3
                        if old >= 0 and old in products[l]:
                            dve.wait_ge(sem("turning"), pbase + products[l].index(old) + 1)
                        elif old < 0:
                            dve.wait_ge(sem("turning"), pbase)
                    dst = soft[s % 3][:, 0:w]
                    if kind == "self" and l == 1 and c == 1:
                        link(dve.tensor_tensor(rden[:, col], rden[:, col], lamv[:, 4:5], ALU.mult))
                        dve.scalar_tensor_tensor(out=dst, in0=prob[s % 3][:, 0:w], scalar=rden[:, col],
                                                 in1=soft[(s - 1) % 3][:, 0:w], op0=ALU.mult, op1=ALU.add)\
                           .then_inc(sem("softened"), 1)
                    else:
                        dve.tensor_scalar(dst, prob[s % 3][:, 0:w], rden[:, col], None, ALU.mult).then_inc(sem("softened"), 1)
                        if kind == "self" and l == 1:
                            dve.wait_ge(sem("softened"), s + 1)

                def head_out(j):
                    if j not in products[l]:
                        return
                    kind, h, n, c = jobs[l][j]
                    m = pbase + products[l].index(j)
                    dve.wait_ge(sem("valued"), m + 1)
                    bank = banks[2 + m % 2]
                    if kind == "mem" or l == 0:
                        lo, tile = (h % 2) * HD, h // 2 + (MIX_HEADS // 2 if kind == "mem" else 0)
                        last = copy(mixT[lo:lo + HD, tile, n * P:(n + 1) * P], bank[lo:lo + HD, 0:P])
                    else:
                        last = copy(heads[:, n, h * P:(h + 1) * P], bank[:, 0:P])
                    last.then_inc(sem("headed"), 1)

                for j in range(J + 3):
                    if j < J:
                        bias(j)
                    if 1 <= j < J + 1:
                        soften(j - 1)
                    if j >= 3:
                        head_out(j - 3)

                if l == 1:
                    dve.wait_ge(sem("headed"), pbase + len(products[l]))
                    hv = heads.rearrange("p t n -> p (t n)")
                    sq = v.rearrange("p t n -> p (t n)")
                    link(dve.tensor_tensor(sq, hv, hv, ALU.mult))
                    dve.tensor_reduce(hsq[:], sq.rearrange("p (h n) -> p h n", n=2 * HD), AX_X, ALU.add).then_inc(sem("head_sq"), 1)
                    dve.wait_ge(sem("head_std"), 1)
                    link(dve.reciprocal(hrstd[:], hstd[:]))
                    h3 = hv.rearrange("p (h n) -> p h n", n=2 * HD)
                    nh = TT * DIFF_HEADS
                    link(dve.tensor_tensor(h3, h3, hrstd[:].rearrange("p (h o) -> p h o", o=1).broadcast_to([P, nh, 2 * HD]), ALU.mult))
                    dve.tensor_tensor(h3, h3, sublnrow[:].rearrange("p (o n) -> p o n", o=1).broadcast_to([P, nh, 2 * HD]), ALU.mult)\
                       .then_inc(sem("heads_normed"), 1)
                    for n in (0, 2):
                        g = G[l, "heads"] + n
                        filled(dve, g)
                        copy(mixT[:, 2 * n:2 * n + 2, :], bank_of(g, 2, SEQ)).then_inc(read, 1)

                for n in range(4):
                    half, t = n // 2, n % 2
                    g = G[l, "y"] + n
                    filled(dve, g)
                    xs = x[:, t, half * 512:half * 512 + 512]
                    dve.scalar_tensor_tensor(out=xs, in0=xs, scalar=ALPHA, in1=banks[g % 4][:], op0=ALU.mult, op1=ALU.add)\
                       .then_inc(read, 1)
                evacuated(dve, G[l, "y"] + 3)
                norm(2 * l, x)
                for n in (0, 2):
                    g = G[l, "xr"] + n
                    filled(dve, g)
                    copy(xT[:, 0:4, n // 2 * P:(n // 2 + 1) * P], bank_of(g, 4, P)).then_inc(read, 1)

                evacuated(dve, G[l, "logit"])
                link(dve.tensor_scalar(aff[:], rsc[:], 1.0, None, ALU.add))
                link(dve.reciprocal(aff[:], aff[:]))
                link(dve.tensor_tensor(sel[:], aff[:], biasrow[:, l:l + 1, :].broadcast_to([P, TT, NE]), ALU.add))
                for t in range(TT):
                    for n in range(NGROUP):
                        last = dve.max(top2[:, t, n, :], sel[:, t, n * PER_GROUP:(n + 1) * PER_GROUP])
                link(last)
                link(dve.tensor_tensor(gsc[:], top2[:, :, :, 0], top2[:, :, :, 1], ALU.add))
                this = gsc[:].rearrange("p t (g o) -> p t g o", o=1).broadcast_to([P, TT, NGROUP, NGROUP])
                for t in range(TT):
                    other = gsc[:, t:t + 1, :].broadcast_to([P, NGROUP, NGROUP])
                    dve.tensor_tensor(cmp1[:, t], other, this[:, t], ALU.is_gt)
                    last = dve.tensor_tensor(cmp2[:, t], other, this[:, t], ALU.is_equal)
                link(last)
                for t in range(TT):
                    last = dve.tensor_tensor(cmp2[:, t], cmp2[:, t], lower[:], ALU.mult)
                link(last)
                link(dve.tensor_tensor(cmp1[:], cmp1[:], cmp2[:], ALU.add))
                link(dve.tensor_reduce(grank[:], cmp1[:], AX_X, ALU.add))
                link(dve.tensor_scalar(gmask[:], grank[:], float(TOPK_GROUPS), None, ALU.is_lt))
                link(dve.tensor_scalar(goff[:], gmask[:], BIG, -BIG, ALU.mult, ALU.add))
                for t in range(TT):
                    grouped = sel[:, t, :].rearrange("p (g e) -> p g e", g=NGROUP)
                    m = gmask[:, t, :].rearrange("p (g o) -> p g o", o=1).broadcast_to([P, NGROUP, PER_GROUP])
                    o = goff[:, t, :].rearrange("p (g o) -> p g o", o=1).broadcast_to([P, NGROUP, PER_GROUP])
                    link(dve.tensor_tensor(grouped, grouped, m, ALU.mult))
                    link(dve.tensor_tensor(grouped, grouped, o, ALU.add))
                for t in range(TT):
                    last = dve.max(top8[:, t, :], sel[:, t, :])
                link(last)
                for t in range(TT):
                    last = dve.match_replace(rsc[:, t, :], top8[:, t, :], sel[:, t, :], -2.0 * BIG)
                link(last)
                dve.tensor_tensor(chosen[:], rsc[:], sel[:], ALU.not_equal).then_inc(sem("chosen"), 1)
                dve.wait_ge(sem("chosen"), l + 1)
                link(dve.tensor_tensor(gate[:], aff[:], chosen[:], ALU.mult))
                link(dve.tensor_reduce(gsum[:], gate[:], AX_X, ALU.add))
                link(dve.reciprocal(grec[:], gsum[:]))
                for t in range(TT):
                    last = dve.tensor_scalar(gate[:, t, :], gate[:, t, :], grec[:, t:t + 1], ROUTED_SCALE, ALU.mult, ALU.mult)
                link(last)
                g = G[l, "hid"] + 1
                evacuated(dve, g - 1)
                filled(dve, g)
                dve.tensor_tensor(hsT, sgs, bank_of(g, FT, SEQ), ALU.mult).then_inc(read, 1)
                g = G[l, "rank"]
                filled(dve, g)
                link(dve.tensor_copy(rank[:], bank_of(g, TT, NE)))
                dve.tensor_reduce(cmax[:], banks[g % 4][:, 2 * NE:3 * NE], AX_X, ALU.max).then_inc(read, 1)
                evacuated(dve, g)
                link(dve.scalar_tensor_tensor(out=rank[:], in0=rank[:], scalar=1.0, in1=chosen[:], op0=ALU.add, op1=ALU.mult))
                link(dve.tensor_scalar(rank[:], rank[:], -1.0, None, ALU.add))
                for n in range(3):
                    last = dve.tensor_scalar(more[:, n:n + 1], cmax[:], float(SLOTS * (n + 1)), None, ALU.is_gt)
                link(last)
                link(dve.tensor_reduce(nround[:], more[:], AX_X, ALU.add))
                dve.tensor_copy(slot_no[:], iota0[:]).then_inc(sem(f"slots_set_{l}"), 1)
                dve.tensor_copy(nround_i[:, l:l + 1], nround[:]).then_inc(sem(f"routed_{l}"), 1)
                dve.wait_ge(sem(f"routed_{l}"), 1)
                for n in range(4):
                    t, half = n // 2, n % 2
                    g = G[l, "down"] + n
                    filled(dve, g)
                    part = slice(half * 512, half * 512 + 512)
                    dve.scalar_tensor_tensor(out=acc[:, t, part], in0=x[:, t, part], scalar=ALPHA, in1=banks[g % 4][:],
                                             op0=ALU.mult, op1=ALU.add).then_inc(read, 1)
                evacuated(dve, G[l, "down"] + 3)

                def s_(name):
                    return sem(f"{name}_{l}")

                def one_hot(U, i, b, r):
                    e = RING * i + 2 * b
                    dve.wait_ge(s_("hot_used"), U + 1)
                    dve.wait_ge(s_("slots_set"), r + 1)
                    shape = [P, TT, 2, SLOTS]
                    slots = slot_no[:].rearrange("p (o u s) -> p o u s", o=1, u=1).broadcast_to(shape)
                    ranks = rank[:, :, bass.ds(e, 2)].rearrange("p t (e o) -> p t e o", o=1).broadcast_to(shape)
                    gates = gate[:, :, bass.ds(e, 2)].rearrange("p t (e o) -> p t e o", o=1).broadcast_to(shape)
                    h4 = hot[b].rearrange("p t (e s) -> p t e s", e=2)
                    dve.tensor_tensor(h4, slots, ranks, ALU.is_equal).then_inc(s_("hot_made"), 1)
                    dve.wait_ge(s_("hot_made"), U + 1)
                    dve.tensor_tensor(hotg[b].rearrange("p t (e s) -> p t e s", e=2), h4, gates, ALU.mult)\
                       .then_inc(s_("hot_ready"), 1)

                def gathered(U, b):
                    dve.wait_ge(s_("gathered"), 2 * U + 2)
                    copy(xg[b][:, 4:8, :], banks[1][:].rearrange("p (k s) -> p k s", k=4)).then_inc(s_("xg_dve"), 1)

                def hidden(U):
                    dve.wait_ge(s_("silu"), U + 1)
                    dve.tensor_tensor(hidrow, sg, banks[2][:, HID:2 * HID], ALU.mult).then_inc(s_("h_ready"), 1)

                def y_out(U):
                    dve.wait_ge(s_("down_done"), 2 * U + 2)
                    copy(y[:, 512:1024], banks[5][:]).then_inc(s_("y_dve"), 1)

                def add(U):
                    for q in range(4):
                        t, half = q // 2, q % 2
                        a = acc[:, t, half * 512:half * 512 + 512]
                        dve.wait_ge(s_("scattered"), 4 * U + q + 1)
                        dve.wait_ge(s_("added"), 4 * U + q + 1)
                        dve.tensor_tensor(a, a, banks[6 + q % 2][:], ALU.add).then_inc(s_("added"), 1)

                def unit(r, i, b, first=False, last=False):
                    U = r * PAIRS + i * UNROLL + b
                    if not last:
                        one_hot(U + 1, i + b, 1 - b, r)
                    hidden(U)
                    if not first:
                        add(U - 1)
                    if not last:
                        gathered(U + 1, 1 - b)
                    y_out(U)

                dve.sem_inc(s_("xg_dve"), 1)
                dve.sem_inc(s_("added"), 4)
                dve.sem_inc(s_("hot_used"), 2)
                rounds = dve.value_load(nround_i[0:1, l:l + 1], min_val=0, max_val=3) + 1
                with dve.Fori(0, rounds) as r:
                    one_hot(r * PAIRS, 0, 0, r)
                    gathered(r * PAIRS, 0)
                    unit(r, 0, 0, first=True)
                    unit(r, 0, 1)
                    with dve.Fori(1, STEPS - 1) as i:
                        unit(r, i, 0)
                        unit(r, i, 1)
                    unit(r, STEPS - 1, 0)
                    unit(r, STEPS - 1, 1, last=True)
                    add(r * PAIRS + PAIRS - 1)
                    dve.tensor_scalar(slot_no[:], slot_no[:], float(SLOTS), None, ALU.add).then_inc(s_("slots_set"), 1)
                dve.wait_ge(s_("added"), (rounds * PAIRS + 1) * 4)
                norm(2 * l + 1, acc)


_INS = ["x", "mem", "w_in_a", "sinks", "w_in_b", "lambda_qk", "subln_g", "w_mem_kv", "w_out", "ln_g", "ln_b", "w_router",
        "router_bias", "w_gate", "w_up", "w_down", "w_shared_gate", "w_shared_up", "w_shared_down"]


def kernel(**inputs):
    import concourse.bacc as bacc
    from concourse.bass_utils import run_bass_kernel_spmd

    nc = bacc.Bacc("TRN2", target_bir_lowering=False, num_devices=1)
    arrays, args = {}, []
    for name in _INS:
        a = np.ascontiguousarray(inputs[name])
        arrays[f"in_{name}"] = a
        args.append(nc.dram_tensor(f"in_{name}", a.shape, mybir.dt.from_np(a.dtype), kind="ExternalInput").ap())
    out = nc.dram_tensor("out_x", (1, SEQ, D), F32, kind="ExternalOutput").ap()
    build_trunk(nc, *args, out)
    r = run_bass_kernel_spmd(nc, [arrays], core_ids=[0])
    return r.results[0]["out_x"]
```

```python
import math
from contextlib import ExitStack

import numpy as np

import concourse.bass as bass
from concourse import mybir

F32 = mybir.dt.float32
BF16 = mybir.dt.bfloat16
I32 = mybir.dt.int32
ALU = mybir.AluOpType
ACT = mybir.ActivationFunctionType
AX_X = mybir.AxisListType.X

P = 128
D = 1024
SEQ = 256
MEM = 256
HD = 64
DEPTH = 2
MEM_HEADS = 4
MIX_HEADS = D // HD - MEM_HEADS
KV_HEADS = MIX_HEADS // 4
DIFF_HEADS = MIX_HEADS // 2
NE = 64
NGROUP = 8
PER_GROUP = NE // NGROUP
TOPK_GROUPS = 4
HID = D // 4
ROUTED_SCALE = 2.5
ALPHA = (2.0 * DEPTH) ** 0.25
LN_EPS = 1e-5
SCALE = HD ** -0.5
WINDOW = 128

KT = D // P
TT = SEQ // P
FT = HID // P
SLOTS = 64
RING = 4
SLOT_F32 = 3 * KT * HID
PAIRS = NE // 2
UNROLL = RING // 2
STEPS = PAIRS // UNROLL
MASKED = -1.0e32
BIG = 1.0e30


def alibi_slopes(n):
    def pow2(m):
        start = 2.0 ** (-8.0 / m)
        return [start ** (i + 1) for i in range(m)]
    if n & (n - 1) == 0:
        s = pow2(n)
    else:
        c = 2 ** int(math.floor(math.log2(n)))
        s = pow2(c) + pow2(2 * c)[0::2][:n - c]
    return [float(v) for v in np.array(s, dtype=np.float32)]


def build_trunk(nc, x_in, mem_in, w_in_a, sinks, w_in_b, lambda_qk, subln_g, w_mem_kv, w_out, ln_g, ln_b,
                w_router, router_bias, w_gate, w_up, w_down, ws_gate, ws_up, ws_down, out):
    slopes = [alibi_slopes(MIX_HEADS), alibi_slopes(DIFF_HEADS)]
    lam_init = 0.8 - 0.6 * math.exp(-0.3 * 1)

    jobs = [
        [("mem", h, n, 0) for h in range(MEM_HEADS) for n in range(TT)]
        + [("self", h, n, 0) for h in range(MIX_HEADS) for n in range(TT)],
        [("mem", h, n, 0) for h in range(MEM_HEADS) for n in range(TT)]
        + [("self", h, n, c) for h in range(DIFF_HEADS) for n in range(TT) for c in range(2)],
    ]

    def keys_of(job):
        return MEM if job[0] == "mem" else (job[2] + 1) * P

    def has_product(layer, job):
        return layer == 0 or job[0] == "mem" or job[3] == 1

    products = [[j for j, job in enumerate(jobs[l]) if has_product(l, job)] for l in range(DEPTH)]

    plan = []
    for l in range(DEPTH):
        plan += [(l, "x", "DADA")] + [(l, "mem", "DADA")] * (l == 0) + [(l, "memkv", "DA")]
        plan += [(l, "q", "DAD"), (l, "k", "AD" if l == 0 else "ADA"), (l, "v", "D" if l == 0 else "DADA"), (l, "qm", "A")]
        plan += [(l, "heads", "DAD")] * (l == 1)
        plan += [(l, "y", "DDDD"), (l, "xr", "DADA"), (l, "logit", "A"), (l, "hid", "AD"), (l, "rank", "D"), (l, "down", "DDDD")]
    G, readers = {}, ""
    for l, name, who in plan:
        G[l, name] = len(readers)
        readers += who

    items = [(0, "memkv"), (0, "in0"), (0, "in1"), (0, "out0"), (0, "out1"), (0, "shared"),
             (1, "memkv"), (1, "in0"), (1, "in1"), (1, "in2"), (1, "in3"), (1, "out0"), (1, "out1"), (1, "shared")]
    pre = [[it for it in items if it[0] == l] for l in range(DEPTH)]
    slot_of = {}
    for l in range(DEPTH):
        first = 0 if l == 0 else len(pre[0])
        for k, it in enumerate(pre[l]):
            slot_of[it] = (first + k) % RING
    expert_slot0 = [len(pre[0]) % RING, (len(pre[0]) + len(pre[1])) % RING]
    assert NE % RING == 0

    with ExitStack() as ctx:
        def sb(name, shape, dt=F32):
            return ctx.enter_context(nc.sbuf_tensor(name, shape, dt))

        named = {}

        def sem(name):
            if name not in named:
                named[name] = ctx.enter_context(nc.semaphore(name))
            return named[name]

        ring = sb("ring", [P, RING, SLOT_F32])
        x = sb("x", [P, TT, D])
        xT = sb("xT", [P, KT, SEQ])
        memT = sb("memT", [P, KT, MEM])
        acc = sb("acc", [P, TT, D])
        lnrow = sb("lnrow", [P, 2, 2, D])
        work = sb("work", [P, 9216])
        qT = work[:, 0:1536].rearrange("p (t n) -> p t n", n=SEQ)
        kT = work[:, 1536:3072].rearrange("p (t n) -> p t n", n=SEQ)
        v = work[:, 3072:4608].rearrange("p (t n) -> p t n", n=768)
        qmT = work[:, 4608:5120].rearrange("p (t n) -> p t n", n=SEQ)
        kmT = work[:, 5120:5632].rearrange("p (t n) -> p t n", n=MEM)
        vm = work[:, 5632:6144].rearrange("p (t n) -> p t n", n=MEM_HEADS * HD)
        mixT = work[:, 6144:8192].rearrange("p (t n) -> p t n", n=SEQ)
        heads = xT[:, 0:6, :].rearrange("p a b -> p (a b)").rearrange("p (t n) -> p t n", n=768)
        memnat = work[:, 0:2048].rearrange("p (t n) -> p t n", n=D)
        xg = [work[:, i * 1024:(i + 1) * 1024].rearrange("p (k s) -> p k s", k=KT) for i in range(2)]
        hidrow = work[:, 2048:2304]
        hT = work[:, 2304:2560].rearrange("p (f s) -> p f s", f=FT)
        sg = work[:, 2560:2816]
        yp = work[:, 3072:4608].bitcast(BF16).rearrange("p (i n) -> p i n", i=3)
        hot = [work[:, 4608 + i * 128:4736 + i * 128].bitcast(BF16).rearrange("p (t s) -> p t s", t=TT) for i in range(2)]
        back = [work[:, 4864 + i * 128:4992 + i * 128].bitcast(BF16).rearrange("p (t n) -> p t n", t=TT) for i in range(2)]
        yrest = work[:, 5120:6144]
        xp = [work[:, 6144 + i * 1024:7168 + i * 1024].bitcast(BF16).rearrange("p (t k c) -> p t k c", t=TT, k=KT) for i in range(3)]
        hsT = work[:, 0:512].rearrange("p (f n) -> p f n", f=FT)
        sgs = work[:, 512:1024].rearrange("p (f n) -> p f n", f=FT)

        scratch = acc[:].rearrange("p t n -> p (t n)")
        score = [scratch[:, i * 257:(i + 1) * 257] for i in range(3)]
        prob = [scratch[:, 771 + i * 257:771 + (i + 1) * 257] for i in range(3)]
        soft = [sb(f"soft{i}", [P, 256]) for i in range(3)]
        softT = [sb(f"softT{i}", [P, 2, P]) for i in range(2)]
        rowmax = sb("rowmax", [P, 32])
        negmax = sb("negmax", [P, 32])
        rowsum = sb("rowsum", [P, 32])
        rden = sb("rden", [P, 32])

        ident = sb("ident", [P, P])
        ident_bf = sb("ident_bf", [P, P], BF16)
        ones = sb("ones", [P, P])
        before = sb("before", [P, P])
        negdist = [sb(f"negdist{l}", [P, 2 * P]) for l in range(DEPTH)]
        iota0 = sb("iota0", [P, SLOTS])
        slot_no = sb("slot_no", [P, SLOTS])
        lower = sb("lower", [P, NGROUP, NGROUP])
        sinkrow = sb("sinkrow", [P, MIX_HEADS])
        biasrow = sb("biasrow", [P, DEPTH, NE])
        lamrow = sb("lamrow", [P, 4, HD])
        sublnrow = sb("sublnrow", [P, 2 * HD])
        lamv = sb("lamv", [P, 8])
        lamp = sb("lamp", [P, 2, HD])
        eps = sb("eps", [P, 1])
        stats = sb("stats", [P, TT, 2, 6])
        mv = sb("mv", [P, TT, 2])
        std = sb("std", [P, TT, 1])
        rstd = sb("rstd", [P, TT, 1])
        hsq = sb("hsq", [P, 12])
        hstd = sb("hstd", [P, 12])
        hrstd = sb("hrstd", [P, 12])
        wr = sb("wr", [P, DEPTH, KT, NE])
        rsc = sb("rsc", [P, TT, NE])
        aff = sb("aff", [P, TT, NE])
        sel = sb("sel", [P, TT, NE])
        top2 = sb("top2", [P, TT, NGROUP, 8])
        gsc = sb("gsc", [P, TT, NGROUP])
        cmp1 = sb("cmp1", [P, TT, NGROUP, NGROUP])
        cmp2 = sb("cmp2", [P, TT, NGROUP, NGROUP])
        grank = sb("grank", [P, TT, NGROUP])
        gmask = sb("gmask", [P, TT, NGROUP])
        goff = sb("goff", [P, TT, NGROUP])
        top8 = sb("top8", [P, TT, 8])
        chosen = sb("chosen", [P, TT, NE])
        gate = sb("gate", [P, TT, NE])
        gparts = sb("gparts", [P, TT, NE, 3], BF16)
        gcol = sb("gcol", [P, 2])
        gsum = sb("gsum", [P, TT])
        grec = sb("grec", [P, TT])
        rank = sb("rank", [P, TT, NE])
        cmax = sb("cmax", [P, 1])
        more = sb("more", [P, 3])
        nround = sb("nround", [P, 1])
        nround_i = sb("nround_i", [P, DEPTH], I32)

        banks = [ctx.enter_context(nc.psum_tensor(f"bank{i}", [P, 512], F32)) for i in range(8)]

        def by_row_run(w):
            return w.rearrange("(p k) n -> p k n", k=KT)

        def item_loads(it):
            l, name = it
            s = ring[:, slot_of[it], :]
            if name == "memkv":
                return [(s[:, 0:KT * 512].rearrange("p (k n) -> p k n", k=KT), by_row_run(w_mem_kv[l]))]
            if name == "shared":
                return expert_loads(s, ws_gate[l], ws_up[l], ws_down[l])
            if name[:3] == "out":
                half = int(name[3])
                src = w_out[l].rearrange("(k p) n -> p k n", p=P)[:, :, half * 512:half * 512 + 512]
                return [(s[:, 0:KT * 512].rearrange("p (k n) -> p k n", k=KT), src)]
            w = by_row_run((w_in_a if l == 0 else w_in_b)[0])
            c0 = int(name[2]) * 768
            n = min(768, w.shape[2] - c0)
            return [(s[:, 0:KT * n].rearrange("p (k n) -> p k n", k=KT), w[:, :, c0:c0 + n])]

        def expert_loads(s, g, u, dn):
            n = KT * HID
            return [(s[:, 0:n].rearrange("p (k n) -> p k n", k=KT), by_row_run(g)),
                    (s[:, n:2 * n].rearrange("p (k n) -> p k n", k=KT), by_row_run(u)),
                    (s[:, 2 * n:3 * n].rearrange("p (f n) -> p f n", f=FT), dn.rearrange("(p f) n -> p f n", f=FT))]

        def item_view(it, n):
            return ring[:, slot_of[it], 0:KT * n].rearrange("p (k n) -> p k n", k=KT)

        def expert_view(slot):
            n = KT * HID
            s = ring[:, slot, :]
            return (s[:, 0:2 * n].rearrange("p (j k f) -> p k j f", j=2, k=KT),
                    s[:, 2 * n:3 * n].rearrange("p (f n) -> p f n", f=FT))

        def last_group(it):
            l, name = it
            phase, n = {"memkv": ("memkv", 1), "in0": ("q", 2), "in1": ("qm", 0) if l == 0 else ("k", 2), "in2": ("v", 3),
                        "in3": ("qm", 0), "out0": ("y", 1), "out1": ("y", 3), "shared": ("down", 3)}[name]
            return G[l, phase] + n

        def landed(eng, it):
            eng.wait_ge(sem(f"landed_{it[1]}_{it[0]}"), 16 * len(item_loads(it)))

        def evacuated(eng, g):
            eng.wait_ge(sem("read_by_" + readers[g]), readers[:g + 1].count(readers[g]))

        def bank_free(pe, g):
            if g >= 4:
                evacuated(pe, g - 4)

        def filled(eng, g):
            eng.wait_ge(sem("group"), g + 1)

        def bank_of(g, n, width):
            return banks[g % 4][:, 0:n * width].rearrange("p (a b) -> p a b", a=n)

        block = ctx.enter_context(nc.Block())

        IDENT = 2
        CONSTS = 14
        ROWS = 4 + DEPTH

        @block.sync
        def _(sp):
            sp.dma_start(x[:], x_in[0].rearrange("(t p) d -> p t d", p=P)).then_inc(sem("x_in"), 16)

            def load(it):
                for dst, src in item_loads(it):
                    sp.dma_start(dst, src).then_inc(sem(f"landed_{it[1]}_{it[0]}"), 16)

            def expert(l, i, k, part):
                slot = (expert_slot0[l] + k) % RING
                e = RING * i + k
                srcs = [w[l, bass.ds(e, 1)].rearrange("a r n -> (a r) n") for w in (w_gate, w_up, w_down)]
                for dst, src in expert_loads(ring[:, slot, :], *srcs)[2 * part:2 * part + 2]:
                    sp.dma_start(dst, src).then_inc(sem(("gate_up_landed", "down_landed")[part] + f"{k}_{l}"), 16)

            def reload(l, units, i, b):
                sp.wait_ge(sem(f"hidden_{l}"), units)
                for k in (2 * b, 2 * b + 1):
                    expert(l, i, k, 0)
                sp.wait_ge(sem(f"down_done_{l}"), 2 * units)
                for k in (2 * b, 2 * b + 1):
                    expert(l, i, k, 1)

            extra = None
            for l in range(DEPTH):
                for k, it in enumerate(pre[l]):
                    if k >= RING:
                        filled(sp, last_group(pre[l][k - RING]))
                    elif l > 0:
                        sp.wait_ge(sem(f"down_done_{l - 1}"), extra * NE + (NE - RING + 2 * (k // 2) + 2))
                    load(it)
                for k in range(RING):
                    filled(sp, last_group(pre[l][len(pre[l]) - RING + k]))
                    expert(l, 0, k, 0)
                    expert(l, 0, k, 1)
                with sp.Fori(0, STEPS - 1) as i:
                    for b in range(UNROLL):
                        reload(l, UNROLL * i + (b + 1), i + 1, b)
                sp.wait_ge(sem(f"routed_{l}"), 1)
                extra = sp.snap(sp.value_load(nround_i[0:1, l:l + 1], min_val=0, max_val=3))
                with sp.If(extra > 0):
                    with sp.Fori(0, extra) as r:
                        with sp.Fori(0, STEPS) as i:
                            for b in range(UNROLL):
                                reload(l, r * PAIRS + UNROLL * i + (PAIRS - UNROLL + b + 1), i, b)
            sp.wait_ge(sem("normed"), 4 * DEPTH)
            sp.dma_start(out[0].rearrange("(t p) d -> p t d", p=P), x[:]).then_inc(sem("out"), 16)
            sp.wait_ge(sem("out"), 16)

        @block.gpsimd
        def _(pool):
            made = sem("const")
            n = 0

            def step(ins):
                nonlocal n
                n += 1
                ins.then_inc(made, 1)
                pool.wait_ge(made, n)

            step(pool.memset(ident[:], 0.0))
            step(pool.affine_select(out=ident[:], in_=ident[:], compare_op=ALU.not_equal, fill=1.0, base=0,
                                    pattern=[[-1, P]], channel_multiplier=1))
            step(pool.tensor_copy(ident_bf[:], ident[:]))
            step(pool.memset(ones[:], 1.0))
            step(pool.affine_select(out=before[:], in_=ones[:], compare_op=ALU.is_gt, fill=0.0, base=0,
                                    pattern=[[1, P]], channel_multiplier=-1))
            for l in range(DEPTH):
                nd = negdist[l]
                step(pool.iota(nd[:], pattern=[[1, 2 * P]], base=-P, channel_multiplier=-1,
                               allow_small_or_imprecise_dtypes=True))
                step(pool.affine_select(out=nd[:], in_=nd[:], compare_op=ALU.is_ge, fill=MASKED, base=P,
                                        pattern=[[-1, 2 * P]], channel_multiplier=1))
                if l == 0:
                    step(pool.affine_select(out=nd[:], in_=nd[:], compare_op=ALU.is_ge, fill=MASKED,
                                            base=WINDOW - 1 - P, pattern=[[1, 2 * P]], channel_multiplier=-1))
            step(pool.iota(iota0[:], pattern=[[1, SLOTS]], base=0, channel_multiplier=0,
                           allow_small_or_imprecise_dtypes=True))
            step(pool.memset(lower[:], 1.0))
            step(pool.affine_select(out=lower[:], in_=lower[:], compare_op=ALU.is_gt, fill=0.0, base=0,
                                    pattern=[[1, NGROUP], [-1, NGROUP]], channel_multiplier=0))
            step(pool.memset(eps[:], LN_EPS))
            assert n == CONSTS

            for l in range(DEPTH):
                base = 0 if l == 0 else len(jobs[0])
                for j in range(len(jobs[l]) + 1):
                    if j < len(jobs[l]) and l == 0:
                        kind, h, n, c = jobs[l][j]
                        w = keys_of(jobs[l][j])
                        if j == 0:
                            pool.wait_ge(sem("rows"), 16 * ROWS)
                        if j >= 3:
                            pool.wait_ge(sem("exped"), j - 2)
                        if kind == "self":
                            pool.tensor_copy(score[j % 3][:, w:w + 1], sinkrow[:, h:h + 1]).then_inc(sem("sink_set"), 1)
                    if j >= 1:
                        kind, h, n, c = jobs[l][j - 1]
                        s, w = base + j - 1, keys_of(jobs[l][j - 1])
                        if kind == "self" and l == 1 and c == 1:
                            continue
                        pool.wait_ge(sem("rden"), s + 1)
                        old = j - 4
                        before_old = [m for m, q in enumerate(products[l]) if q <= old]
                        if s >= 3:
                            pool.wait_ge(sem("turning"), (0 if l == 0 else len(products[0])) + len(before_old))
                            pool.wait_ge(sem("softened"), s - 2)
                        pool.tensor_scalar(soft[s % 3][:, 0:w], prob[s % 3][:, 0:w], rden[:, j - 1:j], None, ALU.mult)\
                            .then_inc(sem("softened"), 1)
                pool.wait_ge(sem("xp0"), l + 1)
                whole = x[:].rearrange("p t (c k) -> p t k c", k=KT)
                rest = acc[:].rearrange("p t (k c) -> p t k c", k=KT)
                parted = sem(f"parted_{l}")
                for t in range(TT):
                    last = pool.tensor_tensor(rest[:, t], whole[:, t], xp[0][:, t], ALU.subtract)
                    last.then_inc(parted, 1)
                pool.wait_ge(parted, 2)
                pool.tensor_copy(xp[1], rest).then_inc(parted, 1)
                pool.wait_ge(parted, 3)
                for t in range(TT):
                    pool.tensor_tensor(xp[2][:, t], rest[:, t], xp[1][:, t], ALU.subtract).then_inc(parted, 1)

        @block.tensor
        def _(pe):
            pe.wait_ge(sem("const"), IDENT)

            def transposes(src, g0, normed):
                for n in range(4):
                    t, half = n // 2, n % 2
                    bank_free(pe, g0 + n)
                    if normed and half == 0:
                        pe.wait_ge(sem("normed"), normed - 1 + t)
                    for k in range(4):
                        last = pe.transpose(banks[(g0 + n) % 4][:, k * P:(k + 1) * P],
                                            src[:, t, 4 * half + k:D:KT], ident[:])
                    last.then_inc(sem("group"), 1)

            def product(dst, pairs):
                for n, (a, b) in enumerate(pairs):
                    last = pe.matmul(dst, a, b, start=(n == 0), stop=(n == len(pairs) - 1))
                return last

            def chunks(w, c0, m, moving):
                return [(w[:, k, c0:c0 + m], moving[:, k, :]) for k in range(KT)]

            def rows(stationary, t, w, c0, n):
                return [(stationary[:, k, t * P:(t + 1) * P], w[:, k, c0:c0 + n]) for k in range(KT)]

            for l in range(DEPTH):
                if l == 0:
                    pe.wait_ge(sem("x_in"), 16)
                transposes(x, G[l, "x"], 4 * l)
                if l == 0:
                    pe.wait_ge(sem("mem_in"), 16)
                    transposes(memnat, G[l, "mem"], 0)
                    for g in range(G[l, "mem"], G[l, "mem"] + 4):
                        evacuated(pe, g)

                g = G[l, "memkv"]
                landed(pe, (l, "memkv"))
                w = item_view((l, "memkv"), 512)
                bank_free(pe, g)
                for c in range(2):
                    last = product(banks[g % 4][:, c * 256:(c + 1) * 256], chunks(w, c * P, P, memT))
                last.then_inc(sem("group"), 1)
                bank_free(pe, g + 1)
                for t in range(2):
                    last = product(banks[(g + 1) % 4][:, t * 256:(t + 1) * 256], rows(memT, t, w, 256, 256))
                last.then_inc(sem("group"), 1)
                for n in range(4):
                    evacuated(pe, G[l, "x"] + n)

                def tile_pair(g, w, c0):
                    bank_free(pe, g)
                    for c in range(2):
                        last = product(banks[g % 4][:, c * 256:(c + 1) * 256], chunks(w, c0 + c * P, P, xT))
                    last.then_inc(sem("group"), 1)

                landed(pe, (l, "in0"))
                for n in range(3):
                    tile_pair(G[l, "q"] + n, item_view((l, "in0"), 768), n * 2 * P)
                landed(pe, (l, "in1"))
                if l == 0:
                    w = item_view((0, "in1"), 640)
                    for n in range(2):
                        g = G[0, "k"] + n
                        m = (2 - n) * HD
                        bank_free(pe, g)
                        product(banks[g % 4][0:m, 0:SEQ], chunks(w, n * 2 * HD, m, xT)).then_inc(sem("group"), 1)
                    g = G[0, "v"]
                    bank_free(pe, g)
                    for t in range(TT):
                        last = product(banks[g % 4][:, t * 192:(t + 1) * 192], rows(xT, t, w, 192, 192))
                    last.then_inc(sem("group"), 1)
                    wm = w[:, :, 384:640]
                else:
                    for n in range(3):
                        tile_pair(G[1, "k"] + n, item_view((1, "in1"), 768), n * 2 * P)
                    landed(pe, (1, "in2"))
                    w = item_view((1, "in2"), 768)
                    for n in range(4):
                        g = G[1, "v"] + n
                        bank_free(pe, g)
                        last = product(banks[g % 4][:, 0:384], rows(xT, n // 2, w, n % 2 * 384, 384))
                        last.then_inc(sem("group"), 1)
                    landed(pe, (1, "in3"))
                    wm = item_view((1, "in3"), 256)
                tile_pair(G[l, "qm"], wm, 0)
                for g in range(G[l, "memkv"], G[l, "qm"] + 1):
                    evacuated(pe, g)

                J = len(jobs[l])
                base = 0 if l == 0 else len(jobs[0])
                pbase = 0 if l == 0 else len(products[0])

                def scores(j):
                    kind, h, n, c = jobs[l][j]
                    s = base + j
                    if s >= 2:
                        pe.wait_ge(sem("score_read"), s - 1)
                    if kind == "mem":
                        lo, tile, ktile, q, kk = (h % 2) * HD, h // 2, h // 2, qmT, kmT
                    elif l == 0:
                        lo, tile, ktile, q, kk = (h % 2) * HD, h // 2, h // 4, qT, kT
                    else:
                        lo, tile, ktile, q, kk = c * HD, h, h, qT, kT
                    pe.matmul(banks[4 + s % 2][:, 0:keys_of(jobs[l][j])], q[lo:lo + HD, tile, n * P:(n + 1) * P],
                              kk[lo:lo + HD, ktile, 0:keys_of(jobs[l][j])], start=True, stop=True)\
                        .then_inc(sem("scored"), 1)

                def turn(j):
                    if j not in products[l]:
                        return
                    s, m = base + j, pbase + products[l].index(j)
                    pe.wait_ge(sem("softened"), s + 1)
                    if m >= 2:
                        pe.wait_ge(sem("turned"), m - 1)
                    for t in range(keys_of(jobs[l][j]) // P):
                        last = pe.transpose(banks[6 + m % 2][:, t * P:(t + 1) * P], soft[s % 3][:, t * P:(t + 1) * P], ident[:])
                    last.then_inc(sem("turning"), 1)

                def values(j):
                    if j not in products[l]:
                        return
                    kind, h, n, c = jobs[l][j]
                    m = pbase + products[l].index(j)
                    pe.wait_ge(sem("turned"), m + 1)
                    if m >= 2:
                        pe.wait_ge(sem("headed"), m - 1)
                    bank = banks[2 + m % 2]
                    nt = keys_of(jobs[l][j]) // P
                    if kind == "mem" or l == 0:
                        lo = (h % 2) * HD
                        col = h * HD if kind == "mem" else (h // 4) * HD
                        vv = vm if kind == "mem" else v
                        last = product(bank[lo:lo + HD, 0:P], [(vv[:, t, col:col + HD], softT[m % 2][:, t, :]) for t in range(nt)])
                    else:
                        last = product(bank[:, 0:P], [(softT[m % 2][:, t, :], v[:, t, h * P:(h + 1) * P]) for t in range(nt)])
                    last.then_inc(sem("valued"), 1)

                for j in range(J + 3):
                    if j < J:
                        scores(j)
                    if 2 <= j < J + 2:
                        turn(j - 2)
                    if j >= 3:
                        values(j - 3)
                pe.wait_ge(sem("headed"), pbase + len(products[l]))

                if l == 1:
                    pe.wait_ge(sem("heads_normed"), 1)
                    g = G[l, "heads"]
                    for n in range(3):
                        bank_free(pe, g + n)
                        for c in range(4):
                            h, t = (4 * n + c) // 2, c % 2
                            last = pe.transpose(banks[(g + n) % 4][:, c * P:(c + 1) * P], heads[:, t, h * P:(h + 1) * P], ident[:])
                        last.then_inc(sem("group"), 1)
                    for n in range(3):
                        evacuated(pe, g + n)

                g = G[l, "y"]
                for half in range(2):
                    it = (l, f"out{half}")
                    landed(pe, it)
                    w = item_view(it, 512)
                    for t in range(TT):
                        bank_free(pe, g + 2 * half + t)
                        last = product(banks[(g + 2 * half + t) % 4][:], rows(mixT, t, w, 0, 512))
                        last.then_inc(sem("group"), 1)

                transposes(x, G[l, "xr"], 4 * l + 2)
                for n in range(4):
                    evacuated(pe, G[l, "xr"] + n)
                g = G[l, "logit"]
                bank_free(pe, g)
                for t in range(TT):
                    last = product(banks[g % 4][:, t * NE:(t + 1) * NE], rows(xT, t, wr[:, l], 0, NE))
                last.then_inc(sem("group"), 1)

                g2 = G[l, "hid"]
                it = (l, "shared")
                landed(pe, it)
                wgu, wd = expert_view(slot_of[it])
                for n in range(2):
                    bank_free(pe, g2 + n)
                    for f in range(FT):
                        last = product(banks[(g2 + n) % 4][:, f * SEQ:(f + 1) * SEQ],
                                       [(wgu[:, k, n, f:HID:FT], xT[:, k, :]) for k in range(KT)])
                    last.then_inc(sem("group"), 1)

                pe.wait_ge(sem("const"), CONSTS)
                pe.wait_ge(sem("chosen"), l + 1)
                g = G[l, "rank"]
                bank_free(pe, g)
                bank = banks[g % 4]
                product(bank[:, 0:NE], [(before[:], chosen[:, 0, :])])
                product(bank[:, NE:2 * NE], [(ones[:], chosen[:, 0, :]), (before[:], chosen[:, 1, :])])
                product(bank[:, 2 * NE:3 * NE], [(ones[:], chosen[:, 0, :]), (ones[:], chosen[:, 1, :])])\
                    .then_inc(sem("group"), 1)

                g = G[l, "down"]
                evacuated(pe, G[l, "hid"] + 1)
                pe.wait_ge(sem("routed_" + str(l)), 1)
                for n in range(4):
                    t, half = n // 2, n % 2
                    bank_free(pe, g + n)
                    last = product(banks[(g + n) % 4][:], [(hsT[:, f, t * P:(t + 1) * P], wd[:, f, half * 512:half * 512 + 512])
                                                           for f in range(FT)])
                    last.then_inc(sem("group"), 1)
                for n in range(4):
                    evacuated(pe, g + n)

                def s_(name):
                    return sem(f"{name}_{l}")

                def front(U, i, b):
                    e = RING * i + 2 * b
                    pe.wait_ge(s_("hot_ready"), U + 1)
                    pe.wait_ge(s_("xg_act"), U + 1)
                    pe.wait_ge(s_("xg_dve"), U + 1)
                    for k in range(KT):
                        last = product(banks[k // 4][:, (k % 4) * P:(k % 4 + 1) * P],
                                       [(part[:, t, k, :], hot[b][:, t, :]) for t in range(TT) for part in xp])
                        if k % 4 == 3:
                            last.then_inc(s_("gathered"), 1)
                    pe.wait_ge(s_("back_ready"), U + 1)
                    pe.wait_ge(s_("gcol_ready"), U + 1)
                    pe.wait_ge(s_("hT_ready"), U + 1)
                    for t in range(TT):
                        pe.transpose(banks[3][:, 256 + t * 64:320 + t * 64].bitcast(BF16), hot[b][:, t, :], ident_bf[:])
                    product(banks[3][:, 384:390],
                            [(hot[b][:, t, :], gparts[:, t, bass.ds(e, 2), :].rearrange("p e i -> p (e i)")) for t in range(TT)])\
                        .then_inc(s_("hot_used"), 1)

                def slots_of(e):
                    return slice(e * SLOTS, (e + 1) * SLOTS)

                def gate_up(U, b, rs):
                    for e in range(2):
                        pe.wait_ge(s_(f"gate_up_landed{2 * b + e}"), rs * 32 + 32)
                    pe.wait_ge(s_("xg_act"), U + 2)
                    pe.wait_ge(s_("xg_dve"), U + 2)
                    w = [expert_view((expert_slot0[l] + 2 * b + e) % RING)[0] for e in range(2)]
                    for k in range(KT):
                        for e in range(2):
                            last = pe.matmul(banks[2][slots_of(e), :], xg[b][:, k, slots_of(e)], w[e][:, k],
                                             start=(k == 0), stop=(k == KT - 1))
                    last.then_inc(s_("hidden"), 1)

                def turn_h(U):
                    pe.wait_ge(s_("h_ready"), U + 1)
                    for f in range(FT):
                        last = pe.transpose(banks[3][:, f * P:(f + 1) * P], hidrow[:, f:HID:FT], ident[:])
                    last.then_inc(s_("h_turned"), 1)

                def down(U, b, rs):
                    for e in range(2):
                        pe.wait_ge(s_(f"down_landed{2 * b + e}"), rs * 16 + 16)
                    pe.wait_ge(s_("hT_ready"), U + 2)
                    w = [expert_view((expert_slot0[l] + 2 * b + e) % RING)[1] for e in range(2)]
                    for half in range(2):
                        for f in range(FT):
                            for e in range(2):
                                last = pe.matmul(banks[4 + half][slots_of(e), :], hT[:, f, slots_of(e)],
                                                 w[e][:, f, half * 512:half * 512 + 512], start=(f == 0), stop=(f == FT - 1))
                        last.then_inc(s_("down_done"), 1)

                def scatter(U, b):
                    pe.wait_ge(s_("y_parted"), 2 * U + 2)
                    for q in range(4):
                        t, half = q // 2, q % 2
                        pe.wait_ge(s_("added"), 4 * U + q + 3)
                        product(banks[6 + q % 2][:], [(back[b][:, t, :], yp[:, n, half * 512:half * 512 + 512]) for n in range(3)])\
                            .then_inc(s_("scattered"), 1)

                def unit(r, i, b, first=False, last=False):
                    U = r * PAIRS + UNROLL * i + b
                    rs = r * STEPS + i
                    gate_up(U, b, rs)
                    if not first:
                        scatter(U - 1, 1 - b)
                    turn_h(U)
                    if not last:
                        front(U + 1, i + b, 1 - b)
                    down(U, b, rs)

                pe.wait_ge(sem(f"parted_{l}"), 5)
                rounds = pe.value_load(nround_i[0:1, l:l + 1], min_val=0, max_val=3) + 1
                with pe.Fori(0, rounds) as r:
                    front(r * PAIRS, 0, 0)
                    unit(r, 0, 0, first=True)
                    unit(r, 0, 1)
                    with pe.Fori(1, STEPS - 1) as i:
                        unit(r, i, 0)
                        unit(r, i, 1)
                    unit(r, STEPS - 1, 0)
                    unit(r, STEPS - 1, 1, last=True)
                    scatter(r * PAIRS + PAIRS - 1, 1)

        def evacuate(eng, me, l, copy, scaled):
            def share(name):
                for n in range(len(readers)):
                    g = G[l, name] + n
                    if (l, name, readers[G[l, name]:g + 1]) not in begun:
                        return
                    if readers[g] == me:
                        filled(eng, g)
                        yield n, g

            begun = {(l_, name, who[:n + 1]) for l_, name, who in plan for n in range(len(who))}
            done = sem("read_by_" + me)
            for name, dst in [("x", xT)] + [("mem", memT)] * (l == 0):
                for n, g in share(name):
                    t, half = n // 2, n % 2
                    copy(dst[:, 4 * half:4 * half + 4, t * P:(t + 1) * P], bank_of(g, 4, P)).then_inc(done, 1)
            for n, g in share("memkv"):
                copy((kmT, vm)[n], bank_of(g, 2, 256)).then_inc(done, 1)
            for n, g in share("q"):
                scaled(qT[:, 2 * n:2 * n + 2, :], bank_of(g, 2, SEQ)).then_inc(done, 1)
            for n, g in share("k"):
                if l == 0:
                    for head in ((0, 1) if n == 0 else (2,)):
                        src = banks[g % 4][head % 2 * HD:(head % 2 + 1) * HD, 0:SEQ]
                        copy(kT[0:HD, head, :], src)
                        last = copy(kT[HD:2 * HD, head, :], src)
                    last.then_inc(done, 1)
                else:
                    copy(kT[:, 2 * n:2 * n + 2, :], bank_of(g, 2, SEQ)).then_inc(done, 1)
            for n, g in share("v"):
                if l == 0:
                    copy(v[:, :, 0:192], bank_of(g, 2, 192)).then_inc(done, 1)
                else:
                    copy(v[:, n // 2, n % 2 * 384:n % 2 * 384 + 384], banks[g % 4][:, 0:384]).then_inc(done, 1)
            for n, g in share("qm"):
                scaled(qmT, bank_of(g, 2, SEQ)).then_inc(done, 1)

        @block.scalar
        def _(act):
            read = sem("read_by_A")
            act.dma_start(memnat, mem_in[0].rearrange("(t p) d -> p t d", p=P)).then_inc(sem("mem_in"), 16)

            def load_norm(n):
                for i, w in enumerate((ln_g, ln_b)):
                    act.dma_start(lnrow[:, n % 2, i, :], w[n // 2, n % 2:n % 2 + 1, :].broadcast_to([P, D]))\
                       .then_inc(sem(f"lnrow{n}"), 16)

            def norm_std(n):
                act.wait_ge(sem("stats"), n + 1)
                for t in range(TT):
                    last = act.activation(std[:, t, :], mv[:, t, 1:2], ACT.Sqrt, bias=eps[:])
                last.then_inc(sem("std"), 1)

            def copy(dst, src):
                return act.activation(dst, src, ACT.Copy)

            def scaled(dst, src):
                return act.activation(dst, src, ACT.Copy, scale=SCALE)

            rows = [(lamrow[:], lambda_qk[0].rearrange("(o a) b -> o a b", o=1).broadcast_to([P, 4, HD])),
                    (sublnrow[:], subln_g.broadcast_to([P, 2 * HD])),
                    (sinkrow[:], sinks.broadcast_to([P, MIX_HEADS])),
                    (biasrow[:], router_bias.rearrange("(o a) b -> o a b", o=1).broadcast_to([P, DEPTH, NE]))]
            rows += [(wr[:, l], by_row_run(w_router[l])) for l in range(DEPTH)]
            assert len(rows) == ROWS
            for dst, src in rows:
                act.dma_start(dst, src).then_inc(sem("rows"), 16)
            load_norm(0)
            load_norm(1)

            for l in range(DEPTH):
                evacuate(act, "A", l, copy, scaled)
                if l == 0:
                    act.wait_ge(sem("lam_sum"), 1)
                    act.activation(lamv[:, 2:4], lamv[:, 0:2], ACT.Exp).then_inc(sem("lam_exp"), 1)

                base = 0 if l == 0 else len(jobs[0])
                pbase = 0 if l == 0 else len(products[0])
                J = len(jobs[l])

                def exps(j):
                    s = base + j
                    w = keys_of(jobs[l][j])
                    act.wait_ge(sem("biased"), s + 1)
                    if s >= 3:
                        act.wait_ge(sem("softened"), s - 2)
                    w += l == 0 and jobs[l][j][0] == "self"
                    act.activation(prob[s % 3][:, 0:w], score[s % 3][:, 0:w], ACT.Exp, bias=negmax[:, j:j + 1],
                                   accum_out=rowsum[:, j:j + 1]).then_inc(sem("exped"), 1)

                def turned(j):
                    if j not in products[l]:
                        return
                    m = pbase + products[l].index(j)
                    nt = keys_of(jobs[l][j]) // P
                    act.wait_ge(sem("turning"), m + 1)
                    if m >= 2:
                        act.wait_ge(sem("valued"), m - 1)
                    copy(softT[m % 2][:, 0:nt, :], banks[6 + m % 2][:, 0:nt * P].rearrange("p (t n) -> p t n", n=P))\
                        .then_inc(sem("turned"), 1)

                def head_out(j):
                    if j not in products[l]:
                        return
                    kind, h, n, c = jobs[l][j]
                    m = pbase + products[l].index(j)
                    act.wait_ge(sem("valued"), m + 1)
                    bank = banks[2 + m % 2]
                    if kind == "mem" or l == 0:
                        lo, tile = (h % 2) * HD, h // 2 + (MIX_HEADS // 2 if kind == "mem" else 0)
                        last = copy(mixT[lo:lo + HD, tile, n * P:(n + 1) * P], bank[lo:lo + HD, 0:P])
                    else:
                        last = copy(heads[:, n, h * P:(h + 1) * P], bank[:, 0:P])
                    last.then_inc(sem("headed"), 1)

                for j in range(J + 3):
                    if j < J:
                        exps(j)
                    if 2 <= j < J + 2:
                        turned(j - 2)
                    if j >= 3:
                        head_out(j - 3)

                if l == 1:
                    act.wait_ge(sem("head_sq"), 1)
                    act.activation(hstd[:], hsq[:], ACT.Sqrt, bias=eps[:], scale=1.0 / (2 * HD)).then_inc(sem("head_std"), 1)
                    g = G[l, "heads"] + 1
                    filled(act, g)
                    copy(mixT[:, 2:4, :], bank_of(g, 2, SEQ)).then_inc(read, 1)
                norm_std(2 * l)
                if l == 0:
                    act.wait_ge(sem("normed"), 2)
                    load_norm(2)
                act.wait_ge(sem("normed"), 4 * l + 2)
                copy(xp[0], x[:].rearrange("p t (c k) -> p t k c", k=KT)).then_inc(sem("xp0"), 1)
                for n in (1, 3):
                    g = G[l, "xr"] + n
                    filled(act, g)
                    copy(xT[:, 4:8, n // 2 * P:(n // 2 + 1) * P], bank_of(g, 4, P)).then_inc(read, 1)
                g = G[l, "logit"]
                filled(act, g)
                act.activation(rsc[:], bank_of(g, TT, NE), ACT.Exp, scale=-1.0).then_inc(read, 1)
                g = G[l, "hid"]
                filled(act, g)
                act.activation(sgs, bank_of(g, FT, SEQ), ACT.Silu).then_inc(read, 1)

                def s_(name):
                    return sem(f"{name}_{l}")

                def silu(U):
                    act.wait_ge(s_("hidden"), U + 1)
                    act.activation(sg, banks[2][:, 0:HID], ACT.Silu).then_inc(s_("silu"), 1)

                def hT_out(U):
                    act.wait_ge(s_("h_turned"), U + 1)
                    copy(hT, banks[3][:, 0:FT * P].rearrange("p (f s) -> p f s", f=FT)).then_inc(s_("hT_ready"), 1)

                def y_out(U, b):
                    act.wait_ge(s_("gcol_ready"), U + 2)
                    for half in range(2):
                        act.wait_ge(s_("down_done"), 2 * U + half + 1)
                        act.activation(yp[:, 0, half * 512:half * 512 + 512], banks[4 + half][:], ACT.Copy,
                                       scale=gcol[:, b:b + 1]).then_inc(s_("y_first"), 1)

                def gathered(U, b):
                    act.wait_ge(s_("gathered"), 2 * U + 1)
                    copy(xg[b][:, 0:4, :], banks[0][:].rearrange("p (k s) -> p k s", k=4)).then_inc(s_("xg_act"), 1)
                    act.wait_ge(s_("hot_used"), U + 3)
                    copy(back[b], banks[3][:, 256:384].bitcast(BF16).rearrange("p (t n) -> p t n", t=TT)).then_inc(s_("back_ready"), 1)

                def unit(r, i, b, first=False, last=False):
                    U = r * PAIRS + i * UNROLL + b
                    silu(U)
                    hT_out(U)
                    if not last:
                        gathered(U + 1, 1 - b)
                    y_out(U, b)

                act.sem_inc(s_("xg_act"), 1)
                act.sem_inc(s_("back_ready"), 1)
                act.sem_inc(s_("hT_ready"), 1)
                act.wait_ge(s_("routed"), 1)
                rounds = act.value_load(nround_i[0:1, l:l + 1], min_val=0, max_val=3) + 1
                with act.Fori(0, rounds) as r:
                    gathered(r * PAIRS, 0)
                    unit(r, 0, 0, first=True)
                    unit(r, 0, 1)
                    with act.Fori(1, STEPS - 1) as i:
                        unit(r, i, 0)
                        unit(r, i, 1)
                    unit(r, STEPS - 1, 0)
                    unit(r, STEPS - 1, 1, last=True)
                norm_std(2 * l + 1)
                if l == 0:
                    act.wait_ge(sem("normed"), 4)
                    load_norm(3)

        @block.vector
        def _(dve):
            read = sem("read_by_D")
            link_count = 0

            def link(ins):
                nonlocal link_count
                link_count += 1
                ins.then_inc(sem("dve_link"), 1)
                dve.wait_ge(sem("dve_link"), link_count)

            def copy(dst, src):
                return dve.tensor_copy(dst, src)

            def scaled(dst, src):
                return dve.tensor_scalar(dst, src, SCALE, None, ALU.mult)

            def statistics(src, t, half):
                return dve.bn_stats(stats[:, t, half, :], src[:, t, half * 512:half * 512 + 512])

            def norm(n, src):
                for t in range(TT):
                    last = dve.bn_aggr(mv[:, t, :], stats[:, t, :, :])
                last.then_inc(sem("stats"), 1)
                dve.wait_ge(sem("std"), n + 1)
                link(dve.reciprocal(rstd[:], std[:]))
                dve.wait_ge(sem(f"lnrow{n}"), 32)
                for t in range(TT):
                    last = dve.tensor_scalar(x[:, t, :], src[:, t, :], mv[:, t, 0:1], rstd[:, t, :], ALU.subtract, ALU.mult)
                link(last)
                for t in range(TT):
                    link(dve.tensor_tensor(x[:, t, :], x[:, t, :], lnrow[:, n % 2, 0, :], ALU.mult))
                    dve.tensor_tensor(x[:, t, :], x[:, t, :], lnrow[:, n % 2, 1, :], ALU.add).then_inc(sem("normed"), 1)

            for l in range(DEPTH):
                evacuate(dve, "D", l, copy, scaled)
                if l == 0:
                    dve.wait_ge(sem("const"), CONSTS)
                    dve.wait_ge(sem("rows"), ROWS * 16)
                    link(dve.tensor_tensor(lamp[:], lamrow[:, 0:4:2, :], lamrow[:, 1:4:2, :], ALU.mult))
                    dve.tensor_reduce(lamv[:, 0:2], lamp[:], AX_X, ALU.add).then_inc(sem("lam_sum"), 1)
                    dve.wait_ge(sem("lam_exp"), 1)
                    dve.scalar_tensor_tensor(out=lamv[:, 4:5], in0=lamv[:, 3:4], scalar=-lam_init, in1=lamv[:, 2:3],
                                             op0=ALU.add, op1=ALU.subtract)
                    link(dve.tensor_scalar(sublnrow[:], sublnrow[:], 1.0 - lam_init, None, ALU.mult))

                base = 0 if l == 0 else len(jobs[0])
                pbase = 0 if l == 0 else len(products[0])
                J = len(jobs[l])

                def bias(j):
                    kind, h, n, c = jobs[l][j]
                    s, w = base + j, keys_of(jobs[l][j])
                    dve.wait_ge(sem("scored"), s + 1)
                    if s >= 3:
                        dve.wait_ge(sem("exped"), s - 2)
                    src, dst = banks[4 + s % 2][:, 0:w], score[s % 3][:, 0:w]
                    if kind == "mem":
                        copy(dst, src).then_inc(sem("score_read"), 1)
                    else:
                        dve.scalar_tensor_tensor(out=dst, in0=negdist[l][:, (1 - n) * P:2 * P], scalar=slopes[l][h], in1=src,
                                                 op0=ALU.mult, op1=ALU.add).then_inc(sem("score_read"), 1)
                    dve.wait_ge(sem("score_read"), s + 1)
                    if kind == "self" and l == 0:
                        dve.wait_ge(sem("sink_set"), j + 1 - TT * MEM_HEADS)
                        dst = score[s % 3][:, 0:w + 1]
                    link(dve.tensor_reduce(rowmax[:, j:j + 1], dst, AX_X, ALU.max))
                    dve.tensor_scalar(negmax[:, j:j + 1], rowmax[:, j:j + 1], -1.0, None, ALU.mult).then_inc(sem("biased"), 1)

                def soften(j):
                    kind, h, n, c = jobs[l][j]
                    s, w = base + j, keys_of(jobs[l][j])
                    col = slice(j, j + 1)
                    dve.wait_ge(sem("exped"), s + 1)
                    dve.reciprocal(rden[:, col], rowsum[:, col]).then_inc(sem("rden"), 1)
                    if kind == "self" and l == 1 and c == 1:
                        dve.wait_ge(sem("rden"), s + 1)
                        link(dve.tensor_tensor(rden[:, col], rden[:, col], lamv[:, 4:5], ALU.mult))
                        dve.wait_ge(sem("turning"), pbase + len([q for q in products[l] if q <= j - 3]))
                        dve.wait_ge(sem("softened"), s)
                        dve.scalar_tensor_tensor(out=soft[s % 3][:, 0:w], in0=prob[s % 3][:, 0:w], scalar=rden[:, col],
                                                 in1=soft[(s - 1) % 3][:, 0:w], op0=ALU.mult, op1=ALU.add)\
                           .then_inc(sem("softened"), 1)

                for j in range(J + 1):
                    if j < J:
                        bias(j)
                    if j >= 1:
                        soften(j - 1)

                if l == 1:
                    dve.wait_ge(sem("headed"), pbase + len(products[l]))
                    hv = heads.rearrange("p t n -> p (t n)")
                    sq = v.rearrange("p t n -> p (t n)")
                    link(dve.tensor_tensor(sq, hv, hv, ALU.mult))
                    dve.tensor_reduce(hsq[:], sq.rearrange("p (h n) -> p h n", n=2 * HD), AX_X, ALU.add).then_inc(sem("head_sq"), 1)
                    dve.wait_ge(sem("head_std"), 1)
                    link(dve.reciprocal(hrstd[:], hstd[:]))
                    h3 = hv.rearrange("p (h n) -> p h n", n=2 * HD)
                    nh = TT * DIFF_HEADS
                    link(dve.tensor_tensor(h3, h3, hrstd[:].rearrange("p (h o) -> p h o", o=1).broadcast_to([P, nh, 2 * HD]), ALU.mult))
                    dve.tensor_tensor(h3, h3, sublnrow[:].rearrange("p (o n) -> p o n", o=1).broadcast_to([P, nh, 2 * HD]), ALU.mult)\
                       .then_inc(sem("heads_normed"), 1)
                    for n in (0, 2):
                        g = G[l, "heads"] + n
                        filled(dve, g)
                        copy(mixT[:, 2 * n:2 * n + 2, :], bank_of(g, 2, SEQ)).then_inc(read, 1)

                for n in range(4):
                    half, t = n // 2, n % 2
                    g = G[l, "y"] + n
                    filled(dve, g)
                    xs = x[:, t, half * 512:half * 512 + 512]
                    dve.scalar_tensor_tensor(out=xs, in0=xs, scalar=ALPHA, in1=banks[g % 4][:], op0=ALU.mult, op1=ALU.add)\
                       .then_inc(read, 1)
                    evacuated(dve, g)
                    last = statistics(x, t, half)
                link(last)
                norm(2 * l, x)
                for n in (0, 2):
                    g = G[l, "xr"] + n
                    filled(dve, g)
                    copy(xT[:, 0:4, n // 2 * P:(n // 2 + 1) * P], bank_of(g, 4, P)).then_inc(read, 1)

                evacuated(dve, G[l, "logit"])
                link(dve.tensor_scalar(aff[:], rsc[:], 1.0, None, ALU.add))
                link(dve.reciprocal(aff[:], aff[:]))
                link(dve.tensor_tensor(sel[:], aff[:], biasrow[:, l:l + 1, :].broadcast_to([P, TT, NE]), ALU.add))
                for t in range(TT):
                    for n in range(NGROUP):
                        last = dve.max(top2[:, t, n, :], sel[:, t, n * PER_GROUP:(n + 1) * PER_GROUP])
                link(last)
                link(dve.tensor_tensor(gsc[:], top2[:, :, :, 0], top2[:, :, :, 1], ALU.add))
                this = gsc[:].rearrange("p t (g o) -> p t g o", o=1).broadcast_to([P, TT, NGROUP, NGROUP])
                for t in range(TT):
                    other = gsc[:, t:t + 1, :].broadcast_to([P, NGROUP, NGROUP])
                    dve.tensor_tensor(cmp1[:, t], other, this[:, t], ALU.is_gt)
                    last = dve.tensor_tensor(cmp2[:, t], other, this[:, t], ALU.is_equal)
                link(last)
                for t in range(TT):
                    last = dve.tensor_tensor(cmp2[:, t], cmp2[:, t], lower[:], ALU.mult)
                link(last)
                link(dve.tensor_tensor(cmp1[:], cmp1[:], cmp2[:], ALU.add))
                link(dve.tensor_reduce(grank[:], cmp1[:], AX_X, ALU.add))
                link(dve.tensor_scalar(gmask[:], grank[:], float(TOPK_GROUPS), None, ALU.is_lt))
                link(dve.tensor_scalar(goff[:], gmask[:], BIG, -BIG, ALU.mult, ALU.add))
                for t in range(TT):
                    grouped = sel[:, t, :].rearrange("p (g e) -> p g e", g=NGROUP)
                    m = gmask[:, t, :].rearrange("p (g o) -> p g o", o=1).broadcast_to([P, NGROUP, PER_GROUP])
                    o = goff[:, t, :].rearrange("p (g o) -> p g o", o=1).broadcast_to([P, NGROUP, PER_GROUP])
                    link(dve.tensor_tensor(grouped, grouped, m, ALU.mult))
                    link(dve.tensor_tensor(grouped, grouped, o, ALU.add))
                for t in range(TT):
                    last = dve.max(top8[:, t, :], sel[:, t, :])
                link(last)
                for t in range(TT):
                    last = dve.match_replace(rsc[:, t, :], top8[:, t, :], sel[:, t, :], -2.0 * BIG)
                link(last)
                dve.tensor_tensor(chosen[:], rsc[:], sel[:], ALU.not_equal).then_inc(sem("chosen"), 1)
                dve.wait_ge(sem("chosen"), l + 1)
                link(dve.tensor_tensor(gate[:], aff[:], chosen[:], ALU.mult))
                link(dve.tensor_reduce(gsum[:], gate[:], AX_X, ALU.add))
                link(dve.reciprocal(grec[:], gsum[:]))
                for t in range(TT):
                    last = dve.tensor_scalar(gate[:, t, :], gate[:, t, :], grec[:, t:t + 1], ROUTED_SCALE, ALU.mult, ALU.mult)
                link(last)
                g = G[l, "hid"] + 1
                evacuated(dve, g - 1)
                filled(dve, g)
                dve.tensor_tensor(hsT, sgs, bank_of(g, FT, SEQ), ALU.mult).then_inc(read, 1)
                gp = [gparts[:, :, :, i] for i in range(3)]
                link(copy(gp[0], gate[:]))
                link(dve.tensor_tensor(gate[:], gate[:], gp[0], ALU.subtract))
                link(copy(gp[1], gate[:]))
                link(dve.tensor_tensor(gp[2], gate[:], gp[1], ALU.subtract))
                g = G[l, "rank"]
                filled(dve, g)
                link(dve.tensor_copy(rank[:], bank_of(g, TT, NE)))
                dve.tensor_reduce(cmax[:], banks[g % 4][:, 2 * NE:3 * NE], AX_X, ALU.max).then_inc(read, 1)
                evacuated(dve, g)
                link(dve.scalar_tensor_tensor(out=rank[:], in0=rank[:], scalar=1.0, in1=chosen[:], op0=ALU.add, op1=ALU.mult))
                link(dve.tensor_scalar(rank[:], rank[:], -1.0, None, ALU.add))
                for n in range(3):
                    last = dve.tensor_scalar(more[:, n:n + 1], cmax[:], float(SLOTS * (n + 1)), None, ALU.is_gt)
                link(last)
                link(dve.tensor_reduce(nround[:], more[:], AX_X, ALU.add))
                dve.tensor_copy(slot_no[:], iota0[:]).then_inc(sem(f"slots_set_{l}"), 1)
                dve.tensor_copy(nround_i[:, l:l + 1], nround[:]).then_inc(sem(f"routed_{l}"), 1)
                dve.wait_ge(sem(f"routed_{l}"), 1)
                dve.wait_ge(sem(f"parted_{l}"), 5)
                for n in range(4):
                    t, half = n // 2, n % 2
                    g = G[l, "down"] + n
                    filled(dve, g)
                    part = slice(half * 512, half * 512 + 512)
                    dve.scalar_tensor_tensor(out=acc[:, t, part], in0=x[:, t, part], scalar=ALPHA, in1=banks[g % 4][:],
                                             op0=ALU.mult, op1=ALU.add).then_inc(read, 1)
                evacuated(dve, G[l, "down"] + 3)

                def s_(name):
                    return sem(f"{name}_{l}")

                def one_hot(U, i, b, r):
                    e = RING * i + 2 * b
                    dve.wait_ge(s_("hot_used"), U + 1)
                    dve.wait_ge(s_("slots_set"), r + 1)
                    shape = [P, TT, 2, SLOTS]
                    slots = slot_no[:].rearrange("p (o u s) -> p o u s", o=1, u=1).broadcast_to(shape)
                    ranks = rank[:, :, bass.ds(e, 2)].rearrange("p t (e o) -> p t e o", o=1).broadcast_to(shape)
                    h4 = hot[b].rearrange("p t (e s) -> p t e s", e=2)
                    dve.tensor_tensor(h4, slots, ranks, ALU.is_equal).then_inc(s_("hot_ready"), 1)

                def gathered(U, b):
                    dve.wait_ge(s_("gathered"), 2 * U + 2)
                    copy(xg[b][:, 4:8, :], banks[1][:].rearrange("p (k s) -> p k s", k=4)).then_inc(s_("xg_dve"), 1)

                def slot_gates(U, b):
                    dve.wait_ge(s_("back_ready"), U + 2)
                    for e in range(2):
                        half = slice(e * SLOTS, (e + 1) * SLOTS)
                        last = dve.tensor_reduce(gcol[half, b:b + 1], banks[3][half, 384 + 3 * e:387 + 3 * e], AX_X, ALU.add)
                    last.then_inc(s_("gcol_ready"), 1)

                def hidden(U):
                    dve.wait_ge(s_("silu"), U + 1)
                    dve.tensor_tensor(hidrow, sg, banks[2][:, HID:2 * HID], ALU.mult).then_inc(s_("h_ready"), 1)

                def y_out(U, b):
                    for half in range(2):
                        part = slice(half * 512, half * 512 + 512)
                        dve.wait_ge(s_("y_first"), 2 * U + half + 1)
                        dve.scalar_tensor_tensor(out=yrest[:, part], in0=banks[4 + half][:], scalar=gcol[:, b:b + 1], in1=yp[:, 0, part],
                                                 op0=ALU.mult, op1=ALU.subtract).then_inc(s_("y_rest"), 1)
                        dve.wait_ge(s_("y_rest"), 2 * U + half + 1)
                        copy(yp[:, 1, part], yrest[:, part]).then_inc(s_("y_second"), 1)
                        dve.wait_ge(s_("y_second"), 2 * U + half + 1)
                        dve.tensor_tensor(yp[:, 2, part], yrest[:, part], yp[:, 1, part], ALU.subtract).then_inc(s_("y_parted"), 1)

                def add(U):
                    for q in range(4):
                        t, half = q // 2, q % 2
                        a = acc[:, t, half * 512:half * 512 + 512]
                        dve.wait_ge(s_("scattered"), 4 * U + q + 1)
                        dve.wait_ge(s_("added"), 4 * U + q + 1)
                        dve.tensor_tensor(a, a, banks[6 + q % 2][:], ALU.add).then_inc(s_("added"), 1)

                def unit(r, i, b, first=False, last=False):
                    U = r * PAIRS + i * UNROLL + b
                    if not last:
                        one_hot(U + 1, i + b, 1 - b, r)
                    hidden(U)
                    if not first:
                        add(U - 1)
                    if not last:
                        gathered(U + 1, 1 - b)
                        slot_gates(U + 1, 1 - b)
                    y_out(U, b)

                dve.sem_inc(s_("gcol_ready"), 1)
                dve.sem_inc(s_("xg_dve"), 1)
                dve.sem_inc(s_("added"), 4)
                dve.sem_inc(s_("hot_used"), 2)
                rounds = dve.value_load(nround_i[0:1, l:l + 1], min_val=0, max_val=3) + 1
                with dve.Fori(0, rounds) as r:
                    one_hot(r * PAIRS, 0, 0, r)
                    gathered(r * PAIRS, 0)
                    slot_gates(r * PAIRS, 0)
                    unit(r, 0, 0, first=True)
                    unit(r, 0, 1)
                    with dve.Fori(1, STEPS - 1) as i:
                        unit(r, i, 0)
                        unit(r, i, 1)
                    unit(r, STEPS - 1, 0)
                    unit(r, STEPS - 1, 1, last=True)
                    add(r * PAIRS + PAIRS - 1)
                    dve.tensor_scalar(slot_no[:], slot_no[:], float(SLOTS), None, ALU.add).then_inc(s_("slots_set"), 1)
                dve.wait_ge(s_("added"), (rounds * PAIRS + 1) * 4)
                for t in range(TT):
                    for half in range(2):
                        last = statistics(acc, t, half)
                link(last)
                norm(2 * l + 1, acc)


_INS = ["x", "mem", "w_in_a", "sinks", "w_in_b", "lambda_qk", "subln_g", "w_mem_kv", "w_out", "ln_g", "ln_b", "w_router",
        "router_bias", "w_gate", "w_up", "w_down", "w_shared_gate", "w_shared_up", "w_shared_down"]


def kernel(**inputs):
    import concourse.bacc as bacc
    from concourse.bass_utils import run_bass_kernel_spmd

    nc = bacc.Bacc("TRN2", target_bir_lowering=False, num_devices=1)
    arrays, args = {}, []
    for name in _INS:
        a = np.ascontiguousarray(inputs[name])
        arrays[f"in_{name}"] = a
        args.append(nc.dram_tensor(f"in_{name}", a.shape, mybir.dt.from_np(a.dtype), kind="ExternalInput").ap())
    out = nc.dram_tensor("out_x", (1, SEQ, D), F32, kind="ExternalOutput").ap()
    build_trunk(nc, *args, out)
    r = run_bass_kernel_spmd(nc, [arrays], core_ids=[0])
    return r.results[0]["out_x"]
```

```python
import math
from contextlib import ExitStack

import numpy as np

import concourse.bass as bass
from concourse import mybir

F32 = mybir.dt.float32
BF16 = mybir.dt.bfloat16
I32 = mybir.dt.int32
ALU = mybir.AluOpType
ACT = mybir.ActivationFunctionType
AX_X = mybir.AxisListType.X

P = 128
D = 1024
SEQ = 256
MEM = 256
HD = 64
DEPTH = 2
MEM_HEADS = 4
MIX_HEADS = D // HD - MEM_HEADS
KV_HEADS = MIX_HEADS // 4
DIFF_HEADS = MIX_HEADS // 2
NE = 64
NGROUP = 8
PER_GROUP = NE // NGROUP
TOPK_GROUPS = 4
HID = D // 4
ROUTED_SCALE = 2.5
ALPHA = (2.0 * DEPTH) ** 0.25
LN_EPS = 1e-5
SCALE = HD ** -0.5
WINDOW = 128

KT = D // P
TT = SEQ // P
FT = HID // P
SLOTS = 64
RING = 4
SLOT_F32 = 3 * KT * HID
PAIRS = NE // 2
UNROLL = RING // 2
STEPS = PAIRS // UNROLL
MASKED = -1.0e32
BIG = 1.0e30
NBUF = 4


def alibi_slopes(n):
    def pow2(m):
        start = 2.0 ** (-8.0 / m)
        return [start ** (i + 1) for i in range(m)]
    if n & (n - 1) == 0:
        s = pow2(n)
    else:
        c = 2 ** int(math.floor(math.log2(n)))
        s = pow2(c) + pow2(2 * c)[0::2][:n - c]
    return [float(v) for v in np.array(s, dtype=np.float32)]


def build_trunk(nc, x_in, mem_in, w_in_a, sinks, w_in_b, lambda_qk, subln_g, w_mem_kv, w_out, ln_g, ln_b,
                w_router, router_bias, w_gate, w_up, w_down, ws_gate, ws_up, ws_down, out):
    slopes = [alibi_slopes(MIX_HEADS), alibi_slopes(DIFF_HEADS)]
    lam_init = 0.8 - 0.6 * math.exp(-0.3 * 1)

    jobs = [
        [(kind, 2 * pair + h, n, 0) for kind, heads in (("mem", MEM_HEADS), ("self", MIX_HEADS))
         for pair in range(heads // 2) for n in range(TT) for h in range(2)],
        [("mem", 2 * pair + h, n, 0) for pair in range(MEM_HEADS // 2) for n in range(TT) for h in range(2)]
        + [("self", h, n, c) for h in range(DIFF_HEADS) for n in range(TT) for c in range(2)],
    ]

    def keys_of(job):
        return MEM if job[0] == "mem" else (job[2] + 1) * P

    def has_product(layer, job):
        return layer == 0 or job[0] == "mem" or job[3] == 1

    products = [[j for j, job in enumerate(jobs[l]) if has_product(l, job)] for l in range(DEPTH)]

    plan = []
    for l in range(DEPTH):
        plan += [(0, "x", "DADA"), (0, "mem", "DADA"), (0, "memkv", "DA")] if l == 0 else [(1, "memkv", "DA"), (1, "x", "DADA")]
        plan += [(l, "q", "DAD"), (l, "k", "AD" if l == 0 else "ADA"), (l, "v", "D" if l == 0 else "DADA"), (l, "qm", "A")]
        plan += [(l, "heads", "DAD")] * (l == 1)
        plan += [(l, "y", "DDD"), (l, "xr0", "AA"), (l, "y3", "D"), (l, "xr1", "DA"), (l, "logit", "A"), (l, "hid", "A"), (l, "rank", "D"), (l, "up", "D"), (l, "down", "DDDD")]
    G, readers = {}, ""
    for l, name, who in plan:
        G[l, name] = len(readers)
        readers += who

    items = [(0, "memkv"), (0, "in0"), (0, "in1"), (0, "out0"), (0, "out1"), (0, "shared"),
             (1, "memkv"), (1, "in0"), (1, "in1"), (1, "in2"), (1, "in3"), (1, "out0"), (1, "out1"), (1, "shared")]
    pre = [[it for it in items if it[0] == l] for l in range(DEPTH)]
    slot_of = {}
    for l in range(DEPTH):
        first = 0 if l == 0 else len(pre[0])
        for k, it in enumerate(pre[l]):
            slot_of[it] = (first + k) % RING
    expert_slot0 = [len(pre[0]) % RING, (len(pre[0]) + len(pre[1])) % RING]
    assert NE % RING == 0

    with ExitStack() as ctx:
        def sb(name, shape, dt=F32):
            return ctx.enter_context(nc.sbuf_tensor(name, shape, dt))

        named = {}

        def sem(name):
            if name not in named:
                named[name] = ctx.enter_context(nc.semaphore(name))
            return named[name]

        ring = sb("ring", [P, RING, SLOT_F32])
        x = sb("x", [P, TT, D])
        xT = sb("xT", [P, KT, SEQ])
        memT = sb("memT", [P, KT, MEM])
        acc = sb("acc", [P, TT, D])
        lnrow = sb("lnrow", [P, 2, 2, D])
        work = sb("work", [P, 9216])
        qT = work[:, 0:1536].rearrange("p (t n) -> p t n", n=SEQ)
        kT = work[:, 1536:3072].rearrange("p (t n) -> p t n", n=SEQ)
        v = work[:, 3072:4608].rearrange("p (t n) -> p t n", n=768)
        qmT = work[:, 4608:5120].rearrange("p (t n) -> p t n", n=SEQ)
        kmT = work[:, 5120:5632].rearrange("p (t n) -> p t n", n=MEM)
        vm = work[:, 5632:6144].rearrange("p (t n) -> p t n", n=MEM_HEADS * HD)
        mixT = work[:, 6144:8192].rearrange("p (t n) -> p t n", n=SEQ)
        heads = xT[:, 0:6, :].rearrange("p a b -> p (a b)").rearrange("p (t n) -> p t n", n=768)
        memnat = work[:, 0:2048].rearrange("p (t n) -> p t n", n=D)
        xg = [work[:, i * 1024:(i + 1) * 1024].rearrange("p (k s) -> p k s", k=KT) for i in range(2)]
        hidrow = work[:, 2048:2304]
        hT = work[:, 2304:2560].rearrange("p (f s) -> p f s", f=FT)
        sg = work[:, 2560:2816]
        yp = work[:, 3072:4608].bitcast(BF16).rearrange("p (i n) -> p i n", i=3)
        hot = [work[:, 4608 + i * 128:4736 + i * 128].bitcast(BF16).rearrange("p (t s) -> p t s", t=TT) for i in range(2)]
        back = [work[:, 4864 + i * 128:4992 + i * 128].bitcast(BF16).rearrange("p (t n) -> p t n", t=TT) for i in range(2)]
        yrest = work[:, 5120:6144]
        xp = [work[:, 6144 + i * 1024:7168 + i * 1024].bitcast(BF16).rearrange("p (t k c) -> p t k c", t=TT, k=KT) for i in range(3)]
        hsT = work[:, 0:512].rearrange("p (f n) -> p f n", f=FT)
        sgs = work[:, 512:1024].rearrange("p (f n) -> p f n", f=FT)

        scratch = acc[:].rearrange("p t n -> p (t n)")
        score = [scratch[:, i * 257:(i + 1) * 257] for i in range(NBUF)]
        prob = [scratch[:, 1028 + i * 257:1028 + (i + 1) * 257] for i in range(3)] + [work[:, 8192:8449]]
        soft = [sb(f"soft{i}", [P, 256]) for i in range(3)] + [work[:, 8450:8706]]
        softT = [sb(f"softT{i}", [P, 2, P]) for i in range(2)]
        rowmax = sb("rowmax", [P, 32])
        negmax = sb("negmax", [P, 32])
        rowsum = sb("rowsum", [P, 32])
        rden = sb("rden", [P, 32])

        ident = sb("ident", [P, P])
        ident_bf = sb("ident_bf", [P, P], BF16)
        ones = sb("ones", [P, P])
        before = sb("before", [P, P])
        negdist = [sb(f"negdist{l}", [P, 2 * P]) for l in range(DEPTH)]
        iota0 = sb("iota0", [P, SLOTS])
        slot_no = sb("slot_no", [P, SLOTS])
        lower = sb("lower", [P, NGROUP, NGROUP])
        sinkrow = sb("sinkrow", [P, MIX_HEADS])
        biasrow = sb("biasrow", [P, DEPTH, NE])
        lamrow = sb("lamrow", [P, 4, HD])
        sublnrow = sb("sublnrow", [P, 2 * HD])
        lamv = sb("lamv", [P, 8])
        lamp = sb("lamp", [P, 2, HD])
        eps = sb("eps", [P, 1])
        stats = sb("stats", [P, TT, 2, 6])
        mv = sb("mv", [P, TT, 2])
        std = sb("std", [P, TT, 1])
        rstd = sb("rstd", [P, TT, 1])
        hsq = sb("hsq", [P, 12])
        square = work[:, 8706:8834]
        hstd = sb("hstd", [P, 12])
        hrstd = sb("hrstd", [P, 12])
        wr = sb("wr", [P, DEPTH, KT, NE])
        rsc = sb("rsc", [P, TT, NE])
        aff = sb("aff", [P, TT, NE])
        sel = sb("sel", [P, TT, NE])
        top2 = sb("top2", [P, TT, NGROUP, 8])
        gsc = sb("gsc", [P, TT, NGROUP])
        cmp1 = sb("cmp1", [P, TT, NGROUP, NGROUP])
        cmp2 = sb("cmp2", [P, TT, NGROUP, NGROUP])
        grank = sb("grank", [P, TT, NGROUP])
        gmask = sb("gmask", [P, TT, NGROUP])
        goff = sb("goff", [P, TT, NGROUP])
        top8 = sb("top8", [P, TT, 8])
        chosen = sb("chosen", [P, TT, NE])
        gate = sb("gate", [P, TT, NE])
        gparts = sb("gparts", [P, TT, NE, 3], BF16)
        gcol = sb("gcol", [P, 2])
        gsum = sb("gsum", [P, TT])
        grec = sb("grec", [P, TT])
        rank = sb("rank", [P, TT, NE])
        cmax = sb("cmax", [P, 1])
        more = sb("more", [P, 3])
        nround = sb("nround", [P, 1])
        nround_i = sb("nround_i", [P, DEPTH], I32)

        banks = [ctx.enter_context(nc.psum_tensor(f"bank{i}", [P, 512], F32)) for i in range(8)]

        def by_row_run(w):
            return w.rearrange("(p k) n -> p k n", k=KT)

        def item_loads(it):
            l, name = it
            s = ring[:, slot_of[it], :]
            if name == "memkv":
                return [(s[:, 0:KT * 512].rearrange("p (k n) -> p k n", k=KT), by_row_run(w_mem_kv[l]))]
            if name == "shared":
                return expert_loads(s, ws_gate[l], ws_up[l], ws_down[l])
            if name[:3] == "out":
                half = int(name[3])
                src = w_out[l].rearrange("(k p) n -> p k n", p=P)[:, :, half * 512:half * 512 + 512]
                return [(s[:, 0:KT * 512].rearrange("p (k n) -> p k n", k=KT), src)]
            w = by_row_run((w_in_a if l == 0 else w_in_b)[0])
            c0 = int(name[2]) * 768
            n = min(768, w.shape[2] - c0)
            return [(s[:, 0:KT * n].rearrange("p (k n) -> p k n", k=KT), w[:, :, c0:c0 + n])]

        def expert_loads(s, g, u, dn):
            n = KT * HID
            return [(s[:, 0:n].rearrange("p (k n) -> p k n", k=KT), by_row_run(g)),
                    (s[:, n:2 * n].rearrange("p (k n) -> p k n", k=KT), by_row_run(u)),
                    (s[:, 2 * n:3 * n].rearrange("p (f n) -> p f n", f=FT), dn.rearrange("(p f) n -> p f n", f=FT))]

        def item_view(it, n):
            return ring[:, slot_of[it], 0:KT * n].rearrange("p (k n) -> p k n", k=KT)

        def expert_view(slot):
            n = KT * HID
            s = ring[:, slot, :]
            return (s[:, 0:2 * n].rearrange("p (j k f) -> p k j f", j=2, k=KT),
                    s[:, 2 * n:3 * n].rearrange("p (f n) -> p f n", f=FT))

        def last_group(it):
            l, name = it
            phase, n = {"memkv": ("memkv", 1), "in0": ("q", 2), "in1": ("qm", 0) if l == 0 else ("k", 2), "in2": ("v", 3),
                        "in3": ("qm", 0), "out0": ("y", 2), "out1": ("y3", 0), "shared": ("down", 3)}[name]
            return G[l, phase] + n

        def landed(eng, it):
            eng.wait_ge(sem(f"landed_{it[1]}_{it[0]}"), 16 * len(item_loads(it)))

        def evacuated(eng, g):
            eng.wait_ge(sem("read_by_" + readers[g]), readers[:g + 1].count(readers[g]))

        def bank_free(pe, g):
            if g >= 4:
                evacuated(pe, g - 4)

        def filled(eng, g):
            eng.wait_ge(sem("group"), g + 1)

        def bank_of(g, n, width):
            return banks[g % 4][:, 0:n * width].rearrange("p (a b) -> p a b", a=n)

        def score_bank(s):
            return banks[(4, 5, 0, 1)[s % 4]]

        block = ctx.enter_context(nc.Block())

        IDENT = 2
        CONSTS = 14
        ROWS = 4 + DEPTH

        @block.sync
        def _(sp):
            sp.dma_start(x[:], x_in[0].rearrange("(t p) d -> p t d", p=P)).then_inc(sem("x_in"), 16)

            def load(it):
                for dst, src in item_loads(it):
                    sp.dma_start(dst, src).then_inc(sem(f"landed_{it[1]}_{it[0]}"), 16)

            def expert(l, i, k, part):
                slot = (expert_slot0[l] + k) % RING
                e = RING * i + k
                srcs = [w[l, bass.ds(e, 1)].rearrange("a r n -> (a r) n") for w in (w_gate, w_up, w_down)]
                for dst, src in expert_loads(ring[:, slot, :], *srcs)[2 * part:2 * part + 2]:
                    sp.dma_start(dst, src).then_inc(sem(("gate_up_landed", "down_landed")[part] + f"{k}_{l}"), 16)

            def reload(l, units, i, b):
                sp.wait_ge(sem(f"hidden_{l}"), units)
                for k in (2 * b, 2 * b + 1):
                    expert(l, i, k, 0)
                sp.wait_ge(sem(f"down_done_{l}"), 2 * units)
                for k in (2 * b, 2 * b + 1):
                    expert(l, i, k, 1)

            extra = None
            for l in range(DEPTH):
                for k, it in enumerate(pre[l]):
                    if k >= RING:
                        filled(sp, last_group(pre[l][k - RING]))
                    elif l > 0:
                        sp.wait_ge(sem(f"down_done_{l - 1}"), extra * NE + (NE - RING + 2 * (k // 2) + 2))
                    load(it)
                for k in range(RING):
                    filled(sp, last_group(pre[l][len(pre[l]) - RING + k]))
                    expert(l, 0, k, 0)
                    expert(l, 0, k, 1)
                with sp.Fori(0, STEPS - 1) as i:
                    for b in range(UNROLL):
                        reload(l, UNROLL * i + (b + 1), i + 1, b)
                sp.wait_ge(sem(f"routed_{l}"), 1)
                extra = sp.snap(sp.value_load(nround_i[0:1, l:l + 1], min_val=0, max_val=3))
                with sp.If(extra > 0):
                    with sp.Fori(0, extra) as r:
                        with sp.Fori(0, STEPS) as i:
                            for b in range(UNROLL):
                                reload(l, r * PAIRS + UNROLL * i + (PAIRS - UNROLL + b + 1), i, b)
            for t in range(TT):
                sp.wait_ge(sem("normed"), 2 * TT * DEPTH - TT + t + 1)
                sp.dma_start(out[0, t * P:(t + 1) * P], x[:, t, :]).then_inc(sem("out"), 16)
            sp.wait_ge(sem("out"), 16 * TT)

        @block.gpsimd
        def _(pool):
            made = sem("const")
            n = 0

            def step(ins):
                nonlocal n
                n += 1
                ins.then_inc(made, 1)
                pool.wait_ge(made, n)

            step(pool.memset(ident[:], 0.0))
            step(pool.affine_select(out=ident[:], in_=ident[:], compare_op=ALU.not_equal, fill=1.0, base=0,
                                    pattern=[[-1, P]], channel_multiplier=1))
            step(pool.tensor_copy(ident_bf[:], ident[:]))
            step(pool.memset(ones[:], 1.0))
            step(pool.affine_select(out=before[:], in_=ones[:], compare_op=ALU.is_gt, fill=0.0, base=0,
                                    pattern=[[1, P]], channel_multiplier=-1))
            for l in range(DEPTH):
                nd = negdist[l]
                step(pool.iota(nd[:], pattern=[[1, 2 * P]], base=-P, channel_multiplier=-1,
                               allow_small_or_imprecise_dtypes=True))
                step(pool.affine_select(out=nd[:], in_=nd[:], compare_op=ALU.is_ge, fill=MASKED, base=P,
                                        pattern=[[-1, 2 * P]], channel_multiplier=1))
                if l == 0:
                    step(pool.affine_select(out=nd[:], in_=nd[:], compare_op=ALU.is_ge, fill=MASKED,
                                            base=WINDOW - 1 - P, pattern=[[1, 2 * P]], channel_multiplier=-1))
            step(pool.iota(iota0[:], pattern=[[1, SLOTS]], base=0, channel_multiplier=0,
                           allow_small_or_imprecise_dtypes=True))
            step(pool.memset(lower[:], 1.0))
            step(pool.affine_select(out=lower[:], in_=lower[:], compare_op=ALU.is_gt, fill=0.0, base=0,
                                    pattern=[[1, NGROUP], [-1, NGROUP]], channel_multiplier=0))
            step(pool.memset(eps[:], LN_EPS))
            assert n == CONSTS

            for l in range(DEPTH):
                base = 0 if l == 0 else len(jobs[0])
                def sink(j):
                    kind, h, n, c = jobs[l][j]
                    if kind == "mem":
                        return
                    w = keys_of(jobs[l][j])
                    pool.wait_ge(sem("exped"), j - NBUF + 1)
                    pool.tensor_copy(score[j % NBUF][:, w:w + 1], sinkrow[:, h:h + 1]).then_inc(sem("sink_set"), 1)

                if l == 0:
                    pool.wait_ge(sem("rows"), 16 * ROWS)
                for j in range(len(jobs[l]) + 1):
                    if l == 0 and j + 2 < len(jobs[l]):
                        sink(j + 2)
                    if j >= 1:
                        kind, h, n, c = jobs[l][j - 1]
                        s, w = base + j - 1, keys_of(jobs[l][j - 1])
                        if kind == "self" and l == 1 and c == 1:
                            continue
                        pool.wait_ge(sem("rden"), s + 1)
                        old = j - 1 - NBUF
                        before_old = [m for m, q in enumerate(products[l]) if q <= old]
                        if s >= NBUF:
                            pool.wait_ge(sem("turning"), (0 if l == 0 else len(products[0])) + len(before_old))
                            pool.wait_ge(sem("softened"), s - 2)
                        pool.tensor_scalar(soft[s % NBUF][:, 0:w], prob[s % NBUF][:, 0:w], rden[:, j - 1:j], None, ALU.mult)\
                            .then_inc(sem("softened"), 1)
                pool.wait_ge(sem("xp0"), l + 1)
                whole = x[:].rearrange("p t (c k) -> p t k c", k=KT)
                rest = acc[:].rearrange("p t (k c) -> p t k c", k=KT)
                parted = sem(f"parted_{l}")
                for t in range(TT):
                    last = pool.tensor_tensor(rest[:, t], whole[:, t], xp[0][:, t], ALU.subtract)
                    last.then_inc(parted, 1)
                pool.wait_ge(parted, 2)
                pool.tensor_copy(xp[1], rest).then_inc(parted, 1)
                pool.wait_ge(parted, 3)
                for t in range(TT):
                    pool.tensor_tensor(xp[2][:, t], rest[:, t], xp[1][:, t], ALU.subtract).then_inc(parted, 1)

        @block.tensor
        def _(pe):
            pe.wait_ge(sem("const"), IDENT)

            def transposes(src, g0, normed, tiles=range(TT)):
                for n, (t, half) in enumerate([(t, half) for t in tiles for half in range(2)]):
                    bank_free(pe, g0 + n)
                    if normed and half == 0:
                        pe.wait_ge(sem("normed"), normed - 1 + t)
                    for k in range(4):
                        last = pe.transpose(banks[(g0 + n) % 4][:, k * P:(k + 1) * P],
                                            src[:, t, 4 * half + k:D:KT], ident[:])
                    last.then_inc(sem("group"), 1)

            def product(dst, pairs):
                for n, (a, b) in enumerate(pairs):
                    last = pe.matmul(dst, a, b, start=(n == 0), stop=(n == len(pairs) - 1))
                return last

            def chunks(w, c0, m, moving):
                return [(w[:, k, c0:c0 + m], moving[:, k, :]) for k in range(KT)]

            def rows(stationary, t, w, c0, n):
                return [(stationary[:, k, t * P:(t + 1) * P], w[:, k, c0:c0 + n]) for k in range(KT)]

            for l in range(DEPTH):
                if l == 0:
                    pe.wait_ge(sem("x_in"), 16)
                    transposes(x, G[l, "x"], 0)
                    pe.wait_ge(sem("mem_in"), 16)
                    transposes(memnat, G[l, "mem"], 0)
                    for g in range(G[l, "mem"], G[l, "mem"] + 4):
                        evacuated(pe, g)

                g = G[l, "memkv"]
                landed(pe, (l, "memkv"))
                w = item_view((l, "memkv"), 512)
                bank_free(pe, g)
                for c in range(2):
                    last = product(banks[g % 4][:, c * 256:(c + 1) * 256], chunks(w, c * P, P, memT))
                last.then_inc(sem("group"), 1)
                bank_free(pe, g + 1)
                for t in range(2):
                    last = product(banks[(g + 1) % 4][:, t * 256:(t + 1) * 256], rows(memT, t, w, 256, 256))
                last.then_inc(sem("group"), 1)
                if l == 1:
                    transposes(x, G[l, "x"], 4 * l)
                for n in range(4):
                    evacuated(pe, G[l, "x"] + n)

                def tile_pair(g, w, c0):
                    bank_free(pe, g)
                    for c in range(2):
                        last = product(banks[g % 4][:, c * 256:(c + 1) * 256], chunks(w, c0 + c * P, P, xT))
                    last.then_inc(sem("group"), 1)

                landed(pe, (l, "in0"))
                for n in range(3):
                    tile_pair(G[l, "q"] + n, item_view((l, "in0"), 768), n * 2 * P)
                landed(pe, (l, "in1"))
                if l == 0:
                    w = item_view((0, "in1"), 640)
                    for n in range(2):
                        g = G[0, "k"] + n
                        m = (2 - n) * HD
                        bank_free(pe, g)
                        product(banks[g % 4][0:m, 0:SEQ], chunks(w, n * 2 * HD, m, xT)).then_inc(sem("group"), 1)
                    g = G[0, "v"]
                    bank_free(pe, g)
                    for t in range(TT):
                        last = product(banks[g % 4][:, t * 192:(t + 1) * 192], rows(xT, t, w, 192, 192))
                    last.then_inc(sem("group"), 1)
                    wm = w[:, :, 384:640]
                else:
                    for n in range(3):
                        tile_pair(G[1, "k"] + n, item_view((1, "in1"), 768), n * 2 * P)
                    landed(pe, (1, "in2"))
                    w = item_view((1, "in2"), 768)
                    for n in range(4):
                        g = G[1, "v"] + n
                        bank_free(pe, g)
                        last = product(banks[g % 4][:, 0:384], rows(xT, n // 2, w, n % 2 * 384, 384))
                        last.then_inc(sem("group"), 1)
                    landed(pe, (1, "in3"))
                    wm = item_view((1, "in3"), 256)
                tile_pair(G[l, "qm"], wm, 0)
                for g in range(G[l, "memkv"], G[l, "qm"] + 1):
                    evacuated(pe, g)

                J = len(jobs[l])
                base = 0 if l == 0 else len(jobs[0])
                pbase = 0 if l == 0 else len(products[0])

                def scores(pair):
                    if base + pair[1] >= 4:
                        pe.wait_ge(sem("score_read"), base + pair[1] - 3)
                    for j in pair:
                        kind, h, n, c = jobs[l][j]
                        if kind == "mem":
                            lo, tile, ktile, q, kk = (h % 2) * HD, h // 2, h // 2, qmT, kmT
                        elif l == 0:
                            lo, tile, ktile, q, kk = (h % 2) * HD, h // 2, h // 4, qT, kT
                        else:
                            lo, tile, ktile, q, kk = c * HD, h, h, qT, kT
                        w = keys_of(jobs[l][j])
                        pe.matmul(score_bank(base + j)[:, 0:w], q[lo:lo + HD, tile, n * P:(n + 1) * P], kk[lo:lo + HD, ktile, 0:w],
                                  start=True, stop=True).then_inc(sem("scored"), 1)

                def turn(j):
                    if j not in products[l]:
                        return
                    s, m = base + j, pbase + products[l].index(j)
                    pe.wait_ge(sem("softened"), s + 1)
                    if m >= 2:
                        pe.wait_ge(sem("turned"), m - 1)
                    for t in range(keys_of(jobs[l][j]) // P):
                        last = pe.transpose(banks[6 + m % 2][:, t * P:(t + 1) * P], soft[s % NBUF][:, t * P:(t + 1) * P], ident[:])
                    last.then_inc(sem("turning"), 1)

                def values(pair):
                    pair = [j for j in pair if j in products[l]]
                    m0 = pbase + products[l].index(pair[0])
                    pe.wait_ge(sem("turned"), m0 + len(pair))
                    if m0 + len(pair) > 2:
                        pe.wait_ge(sem("headed"), m0 + len(pair) - 2)
                    nt = keys_of(jobs[l][pair[0]]) // P
                    for t in range(nt):
                        for i, j in enumerate(pair):
                            kind, h, n, c = jobs[l][j]
                            bank, probs = banks[2 + (m0 + i) % 2], softT[(m0 + i) % 2][:, t, :]
                            if kind == "mem" or l == 0:
                                lo = (h % 2) * HD
                                col = h * HD if kind == "mem" else (h // 4) * HD
                                vv = vm if kind == "mem" else v
                                last = pe.matmul(bank[lo:lo + HD, 0:P], vv[:, t, col:col + HD], probs, start=(t == 0), stop=(t == nt - 1))
                            else:
                                last = pe.matmul(bank[:, 0:P], probs, v[:, t, h * P:(h + 1) * P], start=(t == 0), stop=(t == nt - 1))
                            if t == nt - 1:
                                last.then_inc(sem("valued"), 1)

                job_pairs = [(j, j + 1) for j in range(0, J, 2)]
                for i in range(len(job_pairs) + 3):
                    if i < len(job_pairs):
                        scores(job_pairs[i])
                    if 2 <= i < len(job_pairs) + 2:
                        for j in job_pairs[i - 2]:
                            turn(j)
                    if i >= 3:
                        values(job_pairs[i - 3])
                pe.wait_ge(sem("headed"), pbase + len(products[l]))

                if l == 1:
                    g = G[l, "heads"]
                    for n in range(3):
                        bank_free(pe, g + n)
                        for c in range(4):
                            h, t = (4 * n + c) // 2, c % 2
                            pe.wait_ge(sem("heads_normed"), 4 * n + c + 1)
                            last = pe.transpose(banks[(g + n) % 4][:, c * P:(c + 1) * P], heads[:, t, h * P:(h + 1) * P], ident[:])
                        last.then_inc(sem("group"), 1)
                    for n in range(3):
                        evacuated(pe, g + n)

                for n in range(4):
                    t, half = n // 2, n % 2
                    it = (l, f"out{half}")
                    landed(pe, it)
                    if n == 3:
                        transposes(x, G[l, "xr0"], 4 * l + 2, [0])
                    g = G[l, "y"] + n if n < 3 else G[l, "y3"]
                    bank_free(pe, g)
                    product(banks[g % 4][:], rows(mixT, t, item_view(it, 512), 0, 512)).then_inc(sem("group"), 1)

                g = G[l, "logit"]
                for t in range(TT):
                    if t == 1:
                        transposes(x, G[l, "xr1"], 4 * l + 2, [1])
                    else:
                        bank_free(pe, g)
                    for n in range(2):
                        evacuated(pe, G[l, f"xr{t}"] + n)
                    last = product(banks[g % 4][:, t * NE:(t + 1) * NE], rows(xT, t, wr[:, l], 0, NE))
                last.then_inc(sem("group"), 1)

                it = (l, "shared")
                landed(pe, it)
                wgu, wd = expert_view(slot_of[it])
                def hidden_rows(n):
                    g2 = G[l, ("hid", "up")[n]]
                    bank_free(pe, g2)
                    for f in range(FT):
                        last = product(banks[g2 % 4][:, f * SEQ:(f + 1) * SEQ],
                                       [(wgu[:, k, n, f:HID:FT], xT[:, k, :]) for k in range(KT)])
                    last.then_inc(sem("group"), 1)

                hidden_rows(0)
                pe.wait_ge(sem("const"), CONSTS)
                pe.wait_ge(sem("chosen"), l + 1)
                g = G[l, "rank"]
                bank_free(pe, g)
                bank = banks[g % 4]
                product(bank[:, 0:NE], [(before[:], chosen[:, 0, :])])
                product(bank[:, NE:2 * NE], [(ones[:], chosen[:, 0, :]), (before[:], chosen[:, 1, :])])
                product(bank[:, 2 * NE:3 * NE], [(ones[:], chosen[:, 0, :]), (ones[:], chosen[:, 1, :])])\
                    .then_inc(sem("group"), 1)
                hidden_rows(1)

                g = G[l, "down"]
                evacuated(pe, G[l, "up"])
                pe.wait_ge(sem(f"routed_{l}"), 1)
                rounds = pe.value_load(nround_i[0:1, l:l + 1], min_val=0, max_val=3) + 1
                for n in range(4):
                    t, half = n // 2, n % 2
                    bank_free(pe, g + n)
                    last = product(banks[(g + n) % 4][:], [(hsT[:, f, t * P:(t + 1) * P], wd[:, f, half * 512:half * 512 + 512])
                                                           for f in range(FT)])
                    last.then_inc(sem("group"), 1)
                for n in range(4):
                    evacuated(pe, g + n)

                def s_(name):
                    return sem(f"{name}_{l}")

                def front(U, i, b):
                    e = RING * i + 2 * b
                    pe.wait_ge(s_("hot_ready"), U + 1)
                    pe.wait_ge(s_("xg_act"), U + 1)
                    pe.wait_ge(s_("xg_dve"), U + 1)
                    for k in range(KT):
                        last = product(banks[k // 4][:, (k % 4) * P:(k % 4 + 1) * P],
                                       [(part[:, t, k, :], hot[b][:, t, :]) for t in range(TT) for part in xp])
                        if k % 4 == 3:
                            last.then_inc(s_("gathered"), 1)
                    pe.wait_ge(s_("back_ready"), U + 1)
                    pe.wait_ge(s_("gcol_ready"), U + 1)
                    pe.wait_ge(s_("hT_ready"), U + 1)
                    for t in range(TT):
                        pe.transpose(banks[3][:, 256 + t * 64:320 + t * 64].bitcast(BF16), hot[b][:, t, :], ident_bf[:])
                    product(banks[3][:, 384:390],
                            [(hot[b][:, t, :], gparts[:, t, bass.ds(e, 2), :].rearrange("p e i -> p (e i)")) for t in range(TT)])\
                        .then_inc(s_("hot_used"), 1)

                def slots_of(e):
                    return slice(e * SLOTS, (e + 1) * SLOTS)

                def gate_up(U, b, rs):
                    for e in range(2):
                        pe.wait_ge(s_(f"gate_up_landed{2 * b + e}"), rs * 32 + 32)
                    pe.wait_ge(s_("xg_act"), U + 2)
                    pe.wait_ge(s_("xg_dve"), U + 2)
                    w = [expert_view((expert_slot0[l] + 2 * b + e) % RING)[0] for e in range(2)]
                    for k in range(KT):
                        for e in range(2):
                            last = pe.matmul(banks[2][slots_of(e), :], xg[b][:, k, slots_of(e)], w[e][:, k],
                                             start=(k == 0), stop=(k == KT - 1))
                    last.then_inc(s_("hidden"), 1)

                def turn_h(U):
                    pe.wait_ge(s_("h_ready"), U + 1)
                    for f in range(FT):
                        last = pe.transpose(banks[3][:, f * P:(f + 1) * P], hidrow[:, f:HID:FT], ident[:])
                    last.then_inc(s_("h_turned"), 1)

                def down(U, b, rs):
                    for e in range(2):
                        pe.wait_ge(s_(f"down_landed{2 * b + e}"), rs * 16 + 16)
                    pe.wait_ge(s_("hT_ready"), U + 2)
                    w = [expert_view((expert_slot0[l] + 2 * b + e) % RING)[1] for e in range(2)]
                    for half in range(2):
                        for f in range(FT):
                            for e in range(2):
                                last = pe.matmul(banks[4 + half][slots_of(e), :], hT[:, f, slots_of(e)],
                                                 w[e][:, f, half * 512:half * 512 + 512], start=(f == 0), stop=(f == FT - 1))
                        last.then_inc(s_("down_done"), 1)

                def scatter(U, b, quarters=range(4)):
                    pe.wait_ge(s_("y_parted"), 2 * U + 2)
                    for q in quarters:
                        t, half = q // 2, q % 2
                        pe.wait_ge(s_("added"), 4 * U + q + 3)
                        product(banks[6 + q % 2][:], [(back[b][:, t, :], yp[:, n, half * 512:half * 512 + 512]) for n in range(3)])\
                            .then_inc(s_("scattered"), 1)

                def unit(r, i, b, first=False, last=False):
                    U = r * PAIRS + UNROLL * i + b
                    rs = r * STEPS + i
                    gate_up(U, b, rs)
                    if not first:
                        scatter(U - 1, 1 - b, (0, 1))
                    turn_h(U)
                    if not first:
                        scatter(U - 1, 1 - b, (2, 3))
                    if not last:
                        front(U + 1, i + b, 1 - b)
                    down(U, b, rs)

                pe.wait_ge(sem(f"parted_{l}"), 5)
                with pe.Fori(0, rounds) as r:
                    front(r * PAIRS, 0, 0)
                    unit(r, 0, 0, first=True)
                    unit(r, 0, 1)
                    with pe.Fori(1, STEPS - 1) as i:
                        unit(r, i, 0)
                        unit(r, i, 1)
                    unit(r, STEPS - 1, 0)
                    unit(r, STEPS - 1, 1, last=True)
                    scatter(r * PAIRS + PAIRS - 1, 1)

        def evacuate(eng, me, l, copy, scaled):
            def share(name):
                for n in range(len(readers)):
                    g = G[l, name] + n
                    if (l, name, readers[G[l, name]:g + 1]) not in begun:
                        return
                    if readers[g] == me:
                        filled(eng, g)
                        yield n, g

            begun = {(l_, name, who[:n + 1]) for l_, name, who in plan for n in range(len(who))}
            done = sem("read_by_" + me)
            def turned_rows(name, dst):
                for n, g in share(name):
                    t, half = n // 2, n % 2
                    copy(dst[:, 4 * half:4 * half + 4, t * P:(t + 1) * P], bank_of(g, 4, P)).then_inc(done, 1)

            if l == 0:
                turned_rows("x", xT)
                turned_rows("mem", memT)
            for n, g in share("memkv"):
                copy((kmT, vm)[n], bank_of(g, 2, 256)).then_inc(done, 1)
            if l == 1:
                turned_rows("x", xT)
            for n, g in share("q"):
                scaled(qT[:, 2 * n:2 * n + 2, :], bank_of(g, 2, SEQ)).then_inc(done, 1)
            for n, g in share("k"):
                if l == 0:
                    for head in ((0, 1) if n == 0 else (2,)):
                        src = banks[g % 4][head % 2 * HD:(head % 2 + 1) * HD, 0:SEQ]
                        copy(kT[0:HD, head, :], src)
                        last = copy(kT[HD:2 * HD, head, :], src)
                    last.then_inc(done, 1)
                else:
                    copy(kT[:, 2 * n:2 * n + 2, :], bank_of(g, 2, SEQ)).then_inc(done, 1)
            for n, g in share("v"):
                if l == 0:
                    copy(v[:, :, 0:192], bank_of(g, 2, 192)).then_inc(done, 1)
                else:
                    copy(v[:, n // 2, n % 2 * 384:n % 2 * 384 + 384], banks[g % 4][:, 0:384]).then_inc(done, 1)
            for n, g in share("qm"):
                scaled(qmT, bank_of(g, 2, SEQ)).then_inc(done, 1)

        @block.scalar
        def _(act):
            read = sem("read_by_A")
            act.dma_start(memnat, mem_in[0].rearrange("(t p) d -> p t d", p=P)).then_inc(sem("mem_in"), 16)

            def load_norm(n):
                for i, w in enumerate((ln_g, ln_b)):
                    act.dma_start(lnrow[:, n % 2, i, :], w[n // 2, n % 2:n % 2 + 1, :].broadcast_to([P, D]))\
                       .then_inc(sem(f"lnrow{n}"), 16)

            def norm_std(n, t):
                act.wait_ge(sem("stats"), TT * n + t + 1)
                act.activation(std[:, t, :], mv[:, t, 1:2], ACT.Sqrt, bias=eps[:]).then_inc(sem("std"), 1)

            def copy(dst, src):
                return act.activation(dst, src, ACT.Copy)

            def scaled(dst, src):
                return act.activation(dst, src, ACT.Copy, scale=SCALE)

            rows = [(lamrow[:], lambda_qk[0].rearrange("(o a) b -> o a b", o=1).broadcast_to([P, 4, HD])),
                    (sublnrow[:], subln_g.broadcast_to([P, 2 * HD])),
                    (sinkrow[:], sinks.broadcast_to([P, MIX_HEADS])),
                    (biasrow[:], router_bias.rearrange("(o a) b -> o a b", o=1).broadcast_to([P, DEPTH, NE]))]
            rows += [(wr[:, l], by_row_run(w_router[l])) for l in range(DEPTH)]
            assert len(rows) == ROWS
            for dst, src in rows:
                act.dma_start(dst, src).then_inc(sem("rows"), 16)
            load_norm(0)
            load_norm(1)

            for l in range(DEPTH):
                evacuate(act, "A", l, copy, scaled)
                if l == 0:
                    act.wait_ge(sem("lam_sum"), 1)
                    act.activation(lamv[:, 2:4], lamv[:, 0:2], ACT.Exp).then_inc(sem("lam_exp"), 1)

                base = 0 if l == 0 else len(jobs[0])
                pbase = 0 if l == 0 else len(products[0])
                J = len(jobs[l])

                def exps(j):
                    s = base + j
                    w = keys_of(jobs[l][j])
                    act.wait_ge(sem("biased"), s + 1)
                    if s >= NBUF:
                        act.wait_ge(sem("softened"), s - NBUF + 1)
                    w += l == 0 and jobs[l][j][0] == "self"
                    act.activation(prob[s % NBUF][:, 0:w], score[s % NBUF][:, 0:w], ACT.Exp, bias=negmax[:, j:j + 1],
                                   accum_out=rowsum[:, j:j + 1]).then_inc(sem("exped"), 1)

                def turned(j):
                    if j not in products[l]:
                        return
                    m = pbase + products[l].index(j)
                    nt = keys_of(jobs[l][j]) // P
                    act.wait_ge(sem("turning"), m + 1)
                    if m >= 2:
                        act.wait_ge(sem("valued"), m - 1)
                    copy(softT[m % 2][:, 0:nt, :], banks[6 + m % 2][:, 0:nt * P].rearrange("p (t n) -> p t n", n=P))\
                        .then_inc(sem("turned"), 1)

                def head_out(j):
                    if j not in products[l]:
                        return
                    kind, h, n, c = jobs[l][j]
                    m = pbase + products[l].index(j)
                    act.wait_ge(sem("valued"), m + 1)
                    bank = banks[2 + m % 2]
                    if kind == "mem" or l == 0:
                        lo, tile = (h % 2) * HD, h // 2 + (MIX_HEADS // 2 if kind == "mem" else 0)
                        last = copy(mixT[lo:lo + HD, tile, n * P:(n + 1) * P], bank[lo:lo + HD, 0:P])
                    else:
                        copy(heads[:, n, h * P:(h + 1) * P], bank[:, 0:P])
                        act.wait_ge(sem("headed"), m)
                        last = act.activation(square, bank[:, 0:P], ACT.Square, accum_out=hsq[:, TT * h + n:TT * h + n + 1])
                    last.then_inc(sem("headed"), 1)

                for j in range(J + 6):
                    if 4 <= j < J + 4:
                        turned(j - 4)
                    if j < J:
                        exps(j)
                    if j >= 6:
                        head_out(j - 6)

                if l == 1:
                    act.wait_ge(sem("headed"), pbase + len(products[l]))
                    act.activation(hstd[:], hsq[:], ACT.Sqrt, bias=eps[:], scale=1.0 / (2 * HD)).then_inc(sem("head_std"), 1)
                    g = G[l, "heads"] + 1
                    filled(act, g)
                    copy(mixT[:, 2:4, :], bank_of(g, 2, SEQ)).then_inc(read, 1)
                def turned_x(t, n):
                    g = G[l, f"xr{t}"] + n
                    filled(act, g)
                    copy(xT[:, 4 * n:4 * n + 4, t * P:(t + 1) * P], bank_of(g, 4, P)).then_inc(read, 1)

                norm_std(2 * l, 0)
                turned_x(0, 0)
                turned_x(0, 1)
                norm_std(2 * l, 1)
                turned_x(1, 1)
                act.wait_ge(sem("normed"), 4 * l + 2)
                copy(xp[0], x[:].rearrange("p t (c k) -> p t k c", k=KT)).then_inc(sem("xp0"), 1)
                if l == 0:
                    load_norm(2)
                g = G[l, "logit"]
                filled(act, g)
                act.activation(rsc[:], bank_of(g, TT, NE), ACT.Exp, scale=-1.0).then_inc(read, 1)
                g = G[l, "hid"]
                filled(act, g)
                act.activation(sgs, bank_of(g, FT, SEQ), ACT.Silu).then_inc(read, 1)

                def s_(name):
                    return sem(f"{name}_{l}")

                def silu(U):
                    act.wait_ge(s_("hidden"), U + 1)
                    act.activation(sg, banks[2][:, 0:HID], ACT.Silu).then_inc(s_("silu"), 1)

                def hT_out(U):
                    act.wait_ge(s_("h_turned"), U + 1)
                    copy(hT, banks[3][:, 0:FT * P].rearrange("p (f s) -> p f s", f=FT)).then_inc(s_("hT_ready"), 1)

                def y_out(U, b):
                    act.wait_ge(s_("gcol_ready"), U + 2)
                    for half in range(2):
                        act.wait_ge(s_("down_done"), 2 * U + half + 1)
                        act.activation(yp[:, 0, half * 512:half * 512 + 512], banks[4 + half][:], ACT.Copy,
                                       scale=gcol[:, b:b + 1]).then_inc(s_("y_first"), 1)

                def gathered(U, b):
                    act.wait_ge(s_("gathered"), 2 * U + 1)
                    copy(xg[b][:, 0:4, :], banks[0][:].rearrange("p (k s) -> p k s", k=4)).then_inc(s_("xg_act"), 1)
                    act.wait_ge(s_("hot_used"), U + 3)
                    copy(back[b], banks[3][:, 256:384].bitcast(BF16).rearrange("p (t n) -> p t n", t=TT)).then_inc(s_("back_ready"), 1)

                def unit(r, i, b, first=False, last=False):
                    U = r * PAIRS + i * UNROLL + b
                    silu(U)
                    hT_out(U)
                    if not last:
                        gathered(U + 1, 1 - b)
                    y_out(U, b)

                act.sem_inc(s_("xg_act"), 1)
                act.sem_inc(s_("back_ready"), 1)
                act.sem_inc(s_("hT_ready"), 1)
                act.wait_ge(s_("routed"), 1)
                rounds = act.value_load(nround_i[0:1, l:l + 1], min_val=0, max_val=3) + 1
                with act.Fori(0, rounds) as r:
                    gathered(r * PAIRS, 0)
                    unit(r, 0, 0, first=True)
                    unit(r, 0, 1)
                    with act.Fori(1, STEPS - 1) as i:
                        unit(r, i, 0)
                        unit(r, i, 1)
                    unit(r, STEPS - 1, 0)
                    unit(r, STEPS - 1, 1, last=True)
                for t in range(TT):
                    norm_std(2 * l + 1, t)
                if l == 0:
                    act.wait_ge(sem("normed"), 4)
                    load_norm(3)

        @block.vector
        def _(dve):
            read = sem("read_by_D")
            link_count = 0

            def link(ins):
                nonlocal link_count
                link_count += 1
                ins.then_inc(sem("dve_link"), 1)
                dve.wait_ge(sem("dve_link"), link_count)

            def copy(dst, src):
                return dve.tensor_copy(dst, src)

            def scaled(dst, src):
                return dve.tensor_scalar(dst, src, SCALE, None, ALU.mult)

            def statistics(src, t, half):
                return dve.bn_stats(stats[:, t, half, :], src[:, t, half * 512:half * 512 + 512])

            def norm(n, src, t):
                dve.bn_aggr(mv[:, t, :], stats[:, t, :, :]).then_inc(sem("stats"), 1)
                dve.wait_ge(sem("stats"), TT * n + t + 1)
                dve.wait_ge(sem(f"lnrow{n}"), 32)
                link(dve.scalar_tensor_tensor(out=x[:, t, :], in0=src[:, t, :], scalar=mv[:, t, 0:1], in1=lnrow[:, n % 2, 0, :],
                                              op0=ALU.subtract, op1=ALU.mult))
                dve.wait_ge(sem("std"), TT * n + t + 1)
                link(dve.reciprocal(rstd[:, t, :], std[:, t, :]))
                dve.scalar_tensor_tensor(out=x[:, t, :], in0=x[:, t, :], scalar=rstd[:, t, :], in1=lnrow[:, n % 2, 1, :],
                                         op0=ALU.mult, op1=ALU.add).then_inc(sem("normed"), 1)

            for l in range(DEPTH):
                evacuate(dve, "D", l, copy, scaled)
                if l == 0:
                    dve.wait_ge(sem("const"), CONSTS)
                    dve.wait_ge(sem("rows"), ROWS * 16)
                    link(dve.tensor_tensor(lamp[:], lamrow[:, 0:4:2, :], lamrow[:, 1:4:2, :], ALU.mult))
                    dve.tensor_reduce(lamv[:, 0:2], lamp[:], AX_X, ALU.add).then_inc(sem("lam_sum"), 1)
                    dve.wait_ge(sem("lam_exp"), 1)
                    dve.scalar_tensor_tensor(out=lamv[:, 4:5], in0=lamv[:, 3:4], scalar=-lam_init, in1=lamv[:, 2:3],
                                             op0=ALU.add, op1=ALU.subtract)
                    link(dve.tensor_scalar(sublnrow[:], sublnrow[:], 1.0 - lam_init, None, ALU.mult))

                base = 0 if l == 0 else len(jobs[0])
                pbase = 0 if l == 0 else len(products[0])
                J = len(jobs[l])

                def bias(j):
                    kind, h, n, c = jobs[l][j]
                    s, w = base + j, keys_of(jobs[l][j])
                    dve.wait_ge(sem("scored"), s + 1)
                    if s >= NBUF:
                        dve.wait_ge(sem("exped"), s - NBUF + 1)
                    src, dst = score_bank(s)[:, 0:w], score[s % NBUF][:, 0:w]
                    if kind == "mem":
                        copy(dst, src).then_inc(sem("score_read"), 1)
                    else:
                        dve.scalar_tensor_tensor(out=dst, in0=negdist[l][:, (1 - n) * P:2 * P], scalar=slopes[l][h], in1=src,
                                                 op0=ALU.mult, op1=ALU.add).then_inc(sem("score_read"), 1)
                    dve.wait_ge(sem("score_read"), s + 1)
                    if kind == "self" and l == 0:
                        dve.wait_ge(sem("sink_set"), j + 1 - TT * MEM_HEADS)
                        dst = score[s % NBUF][:, 0:w + 1]
                    link(dve.tensor_reduce(rowmax[:, j:j + 1], dst, AX_X, ALU.max))
                    dve.tensor_scalar(negmax[:, j:j + 1], rowmax[:, j:j + 1], -1.0, None, ALU.mult).then_inc(sem("biased"), 1)

                def soften(j):
                    kind, h, n, c = jobs[l][j]
                    s, w = base + j, keys_of(jobs[l][j])
                    col = slice(j, j + 1)
                    dve.wait_ge(sem("exped"), s + 1)
                    dve.reciprocal(rden[:, col], rowsum[:, col]).then_inc(sem("rden"), 1)
                    if kind == "self" and l == 1 and c == 1:
                        dve.wait_ge(sem("rden"), s + 1)
                        link(dve.tensor_tensor(rden[:, col], rden[:, col], lamv[:, 4:5], ALU.mult))
                        dve.wait_ge(sem("turning"), pbase + len([q for q in products[l] if q <= j - NBUF]))
                        dve.wait_ge(sem("softened"), s)
                        dve.scalar_tensor_tensor(out=soft[s % NBUF][:, 0:w], in0=prob[s % NBUF][:, 0:w], scalar=rden[:, col],
                                                 in1=soft[(s - 1) % NBUF][:, 0:w], op0=ALU.mult, op1=ALU.add)\
                           .then_inc(sem("softened"), 1)

                for j in range(J + 1):
                    if j < J:
                        bias(j)
                    if j >= 1:
                        soften(j - 1)

                if l == 1:
                    dve.wait_ge(sem("headed"), pbase + len(products[l]))
                    dve.wait_ge(sem("head_std"), 1)
                    link(dve.reciprocal(hrstd[:], hstd[:]))
                    for h in range(DIFF_HEADS):
                        for t in range(TT):
                            hd = heads[:, t, h * P:(h + 1) * P]
                            dve.scalar_tensor_tensor(out=hd, in0=hd, scalar=hrstd[:, TT * h + t:TT * h + t + 1], in1=sublnrow[:],
                                                     op0=ALU.mult, op1=ALU.mult).then_inc(sem("heads_normed"), 1)
                    for n in (0, 2):
                        g = G[l, "heads"] + n
                        filled(dve, g)
                        copy(mixT[:, 2 * n:2 * n + 2, :], bank_of(g, 2, SEQ)).then_inc(read, 1)

                for n in range(4):
                    t, half = n // 2, n % 2
                    g = G[l, "y"] + n if n < 3 else G[l, "y3"]
                    filled(dve, g)
                    xs = x[:, t, half * 512:half * 512 + 512]
                    dve.scalar_tensor_tensor(out=xs, in0=xs, scalar=ALPHA, in1=banks[g % 4][:], op0=ALU.mult, op1=ALU.add)\
                       .then_inc(read, 1)
                    evacuated(dve, g)
                    last = statistics(x, t, half)
                    if half == 1:
                        link(last)
                        norm(2 * l, x, t)
                g = G[l, "xr1"]
                filled(dve, g)
                copy(xT[:, 0:4, P:2 * P], bank_of(g, 4, P)).then_inc(read, 1)

                evacuated(dve, G[l, "logit"])
                link(dve.tensor_scalar(aff[:], rsc[:], 1.0, None, ALU.add))
                link(dve.reciprocal(aff[:], aff[:]))
                link(dve.tensor_tensor(sel[:], aff[:], biasrow[:, l:l + 1, :].broadcast_to([P, TT, NE]), ALU.add))
                for t in range(TT):
                    for n in range(NGROUP):
                        last = dve.max(top2[:, t, n, :], sel[:, t, n * PER_GROUP:(n + 1) * PER_GROUP])
                link(last)
                link(dve.tensor_tensor(gsc[:], top2[:, :, :, 0], top2[:, :, :, 1], ALU.add))
                this = gsc[:].rearrange("p t (g o) -> p t g o", o=1).broadcast_to([P, TT, NGROUP, NGROUP])
                for t in range(TT):
                    other = gsc[:, t:t + 1, :].broadcast_to([P, NGROUP, NGROUP])
                    dve.tensor_tensor(cmp1[:, t], other, this[:, t], ALU.is_gt)
                    last = dve.tensor_tensor(cmp2[:, t], other, this[:, t], ALU.is_equal)
                link(last)
                for t in range(TT):
                    last = dve.tensor_tensor(cmp2[:, t], cmp2[:, t], lower[:], ALU.mult)
                link(last)
                link(dve.tensor_tensor(cmp1[:], cmp1[:], cmp2[:], ALU.add))
                link(dve.tensor_reduce(grank[:], cmp1[:], AX_X, ALU.add))
                link(dve.tensor_scalar(gmask[:], grank[:], float(TOPK_GROUPS), None, ALU.is_lt))
                link(dve.tensor_scalar(goff[:], gmask[:], BIG, -BIG, ALU.mult, ALU.add))
                for t in range(TT):
                    grouped = sel[:, t, :].rearrange("p (g e) -> p g e", g=NGROUP)
                    m = gmask[:, t, :].rearrange("p (g o) -> p g o", o=1).broadcast_to([P, NGROUP, PER_GROUP])
                    o = goff[:, t, :].rearrange("p (g o) -> p g o", o=1).broadcast_to([P, NGROUP, PER_GROUP])
                    link(dve.tensor_tensor(grouped, grouped, m, ALU.mult))
                    link(dve.tensor_tensor(grouped, grouped, o, ALU.add))
                for t in range(TT):
                    last = dve.max(top8[:, t, :], sel[:, t, :])
                link(last)
                for t in range(TT):
                    last = dve.match_replace(rsc[:, t, :], top8[:, t, :], sel[:, t, :], -2.0 * BIG)
                link(last)
                dve.tensor_tensor(chosen[:], rsc[:], sel[:], ALU.not_equal).then_inc(sem("chosen"), 1)
                dve.wait_ge(sem("chosen"), l + 1)
                link(dve.tensor_tensor(gate[:], aff[:], chosen[:], ALU.mult))
                link(dve.tensor_reduce(gsum[:], gate[:], AX_X, ALU.add))
                link(dve.reciprocal(grec[:], gsum[:]))
                for t in range(TT):
                    last = dve.tensor_scalar(gate[:, t, :], gate[:, t, :], grec[:, t:t + 1], ROUTED_SCALE, ALU.mult, ALU.mult)
                link(last)
                gp = [gparts[:, :, :, i] for i in range(3)]
                link(copy(gp[0], gate[:]))
                link(dve.tensor_tensor(gate[:], gate[:], gp[0], ALU.subtract))
                link(copy(gp[1], gate[:]))
                link(dve.tensor_tensor(gp[2], gate[:], gp[1], ALU.subtract))
                g = G[l, "rank"]
                filled(dve, g)
                link(dve.tensor_copy(rank[:], bank_of(g, TT, NE)))
                dve.tensor_reduce(cmax[:], banks[g % 4][:, 2 * NE:3 * NE], AX_X, ALU.max).then_inc(read, 1)
                evacuated(dve, g)
                link(dve.scalar_tensor_tensor(out=rank[:], in0=rank[:], scalar=1.0, in1=chosen[:], op0=ALU.add, op1=ALU.mult))
                link(dve.tensor_scalar(rank[:], rank[:], -1.0, None, ALU.add))
                for n in range(3):
                    last = dve.tensor_scalar(more[:, n:n + 1], cmax[:], float(SLOTS * (n + 1)), None, ALU.is_gt)
                link(last)
                link(dve.tensor_reduce(nround[:], more[:], AX_X, ALU.add))
                dve.tensor_copy(slot_no[:], iota0[:]).then_inc(sem(f"slots_set_{l}"), 1)
                dve.tensor_copy(nround_i[:, l:l + 1], nround[:]).then_inc(sem(f"routed_{l}"), 1)
                dve.wait_ge(sem(f"routed_{l}"), 1)
                g = G[l, "up"]
                evacuated(dve, G[l, "hid"])
                filled(dve, g)
                dve.tensor_tensor(hsT, sgs, bank_of(g, FT, SEQ), ALU.mult).then_inc(read, 1)
                rounds = dve.value_load(nround_i[0:1, l:l + 1], min_val=0, max_val=3) + 1
                dve.wait_ge(sem(f"parted_{l}"), 5)
                for n in range(4):
                    t, half = n // 2, n % 2
                    g = G[l, "down"] + n
                    filled(dve, g)
                    part = slice(half * 512, half * 512 + 512)
                    dve.scalar_tensor_tensor(out=acc[:, t, part], in0=x[:, t, part], scalar=ALPHA, in1=banks[g % 4][:],
                                             op0=ALU.mult, op1=ALU.add).then_inc(read, 1)
                evacuated(dve, G[l, "down"] + 3)

                def s_(name):
                    return sem(f"{name}_{l}")

                def one_hot(U, i, b, r):
                    e = RING * i + 2 * b
                    dve.wait_ge(s_("hot_used"), U + 1)
                    dve.wait_ge(s_("slots_set"), r + 1)
                    shape = [P, TT, 2, SLOTS]
                    slots = slot_no[:].rearrange("p (o u s) -> p o u s", o=1, u=1).broadcast_to(shape)
                    ranks = rank[:, :, bass.ds(e, 2)].rearrange("p t (e o) -> p t e o", o=1).broadcast_to(shape)
                    h4 = hot[b].rearrange("p t (e s) -> p t e s", e=2)
                    dve.tensor_tensor(h4, slots, ranks, ALU.is_equal).then_inc(s_("hot_ready"), 1)

                def gathered(U, b):
                    dve.wait_ge(s_("gathered"), 2 * U + 2)
                    copy(xg[b][:, 4:8, :], banks[1][:].rearrange("p (k s) -> p k s", k=4)).then_inc(s_("xg_dve"), 1)

                def slot_gates(U, b):
                    dve.wait_ge(s_("back_ready"), U + 2)
                    for e in range(2):
                        half = slice(e * SLOTS, (e + 1) * SLOTS)
                        last = dve.tensor_reduce(gcol[half, b:b + 1], banks[3][half, 384 + 3 * e:387 + 3 * e], AX_X, ALU.add)
                    last.then_inc(s_("gcol_ready"), 1)

                def hidden(U):
                    dve.wait_ge(s_("silu"), U + 1)
                    dve.tensor_tensor(hidrow, sg, banks[2][:, HID:2 * HID], ALU.mult).then_inc(s_("h_ready"), 1)

                def y_out(U, b):
                    for half in range(2):
                        part = slice(half * 512, half * 512 + 512)
                        dve.wait_ge(s_("y_first"), 2 * U + half + 1)
                        dve.scalar_tensor_tensor(out=yrest[:, part], in0=banks[4 + half][:], scalar=gcol[:, b:b + 1], in1=yp[:, 0, part],
                                                 op0=ALU.mult, op1=ALU.subtract).then_inc(s_("y_rest"), 1)
                        dve.wait_ge(s_("y_rest"), 2 * U + half + 1)
                        copy(yp[:, 1, part], yrest[:, part]).then_inc(s_("y_second"), 1)
                        dve.wait_ge(s_("y_second"), 2 * U + half + 1)
                        dve.tensor_tensor(yp[:, 2, part], yrest[:, part], yp[:, 1, part], ALU.subtract).then_inc(s_("y_parted"), 1)

                def add(U):
                    for q in range(4):
                        t, half = q // 2, q % 2
                        a = acc[:, t, half * 512:half * 512 + 512]
                        dve.wait_ge(s_("scattered"), 4 * U + q + 1)
                        dve.wait_ge(s_("added"), 4 * U + q + 1)
                        dve.tensor_tensor(a, a, banks[6 + q % 2][:], ALU.add).then_inc(s_("added"), 1)

                def unit(r, i, b, first=False, last=False):
                    U = r * PAIRS + i * UNROLL + b
                    if not last:
                        one_hot(U + 1, i + b, 1 - b, r)
                    hidden(U)
                    if not first:
                        add(U - 1)
                    if not last:
                        gathered(U + 1, 1 - b)
                        slot_gates(U + 1, 1 - b)
                    y_out(U, b)

                dve.sem_inc(s_("gcol_ready"), 1)
                dve.sem_inc(s_("xg_dve"), 1)
                dve.sem_inc(s_("added"), 4)
                dve.sem_inc(s_("hot_used"), 2)
                with dve.Fori(0, rounds) as r:
                    one_hot(r * PAIRS, 0, 0, r)
                    gathered(r * PAIRS, 0)
                    slot_gates(r * PAIRS, 0)
                    unit(r, 0, 0, first=True)
                    unit(r, 0, 1)
                    with dve.Fori(1, STEPS - 1) as i:
                        unit(r, i, 0)
                        unit(r, i, 1)
                    unit(r, STEPS - 1, 0)
                    unit(r, STEPS - 1, 1, last=True)
                    add(r * PAIRS + PAIRS - 1)
                    dve.tensor_scalar(slot_no[:], slot_no[:], float(SLOTS), None, ALU.add).then_inc(s_("slots_set"), 1)
                dve.wait_ge(s_("added"), (rounds * PAIRS + 1) * 4)
                for t in range(TT):
                    for half in range(2):
                        last = statistics(acc, t, half)
                    link(last)
                    norm(2 * l + 1, acc, t)


_INS = ["x", "mem", "w_in_a", "sinks", "w_in_b", "lambda_qk", "subln_g", "w_mem_kv", "w_out", "ln_g", "ln_b", "w_router",
        "router_bias", "w_gate", "w_up", "w_down", "w_shared_gate", "w_shared_up", "w_shared_down"]


def kernel(**inputs):
    import concourse.bacc as bacc
    from concourse.bass_utils import run_bass_kernel_spmd

    nc = bacc.Bacc("TRN2", target_bir_lowering=False, num_devices=1)
    arrays, args = {}, []
    for name in _INS:
        a = np.ascontiguousarray(inputs[name])
        arrays[f"in_{name}"] = a
        args.append(nc.dram_tensor(f"in_{name}", a.shape, mybir.dt.from_np(a.dtype), kind="ExternalInput").ap())
    out = nc.dram_tensor("out_x", (1, SEQ, D), F32, kind="ExternalOutput").ap()
    build_trunk(nc, *args, out)
    r = run_bass_kernel_spmd(nc, [arrays], core_ids=[0])
    return r.results[0]["out_x"]
```
